# Optimizing a Trainium2 kernel written in Bass

```python
import jax, jax.numpy as jnp
from jax import lax
import numpy as np

D_MODEL = 2048
BATCH = 1
SEQ = 256
DEPTH = 1

EPS = 1e-6
SSM_D_INNER = 2048
SSM_HEAD_DIM = 64
SSM_HEADS = SSM_D_INNER // SSM_HEAD_DIM
SSM_GROUPS = 8
SSM_STATE = 128
SSM_CONV_K = 5
SSM_CHUNK = 128
SSM_XBC = SSM_D_INNER + 2 * SSM_GROUPS * SSM_STATE
ATTN_HEAD_DIM = 128
ATTN_Q_HEADS = 16
ATTN_KV_HEADS = 4
ATTN_Q_BLOCK = 128
ROPE_THETA = 10000.0
GRID_W = 64
D_FF = 4 * D_MODEL
IN_SIZES = (SSM_D_INNER, SSM_XBC, SSM_HEADS, SSM_HEADS,
            ATTN_Q_HEADS * ATTN_HEAD_DIM, ATTN_KV_HEADS * ATTN_HEAD_DIM, ATTN_KV_HEADS * ATTN_HEAD_DIM,
            D_MODEL, D_MODEL)
N_IN = sum(IN_SIZES)

kernel_name = "hybrid_ssd_axial_gqa_gated_encoder"

def rms_norm(x, g):
    xf = x.astype(jnp.float32)
    y = xf * lax.rsqrt(jnp.mean(xf * xf, axis=-1, keepdims=True) + EPS)
    return (y * g.astype(jnp.float32)).astype(x.dtype)

def split_points(sizes):
    pts, acc = [], 0
    for s in sizes[:-1]:
        acc += s
        pts.append(acc)
    return pts

def centred_depthwise_conv(u, w, b):
    c = u.shape[-1]
    k = w.shape[0]
    out = lax.conv_general_dilated(
        u, w.reshape(k, 1, c).astype(u.dtype), window_strides=(1,),
        padding=[(k // 2, k // 2)], dimension_numbers=("NWC", "WIO", "NWC"),
        feature_group_count=c)
    return out + b.astype(u.dtype)

def ssd_scan(xh, a, bg, cg, chunk):
    b, s, h, p = xh.shape
    g, n = bg.shape[-2:]
    r = h // g
    c = s // chunk
    x = xh.reshape(b, c, chunk, g, r, p)
    a = a.reshape(b, c, chunk, g, r)
    bm = bg.reshape(b, c, chunk, g, n)
    cm = cg.reshape(b, c, chunk, g, n)
    a_cum = jnp.cumsum(a, axis=2)
    seg = a_cum[:, :, :, None] - a_cum[:, :, None, :]
    mask = jnp.tril(jnp.ones((chunk, chunk), dtype=bool))[:, :, None, None]
    decay = jnp.exp(jnp.where(mask, seg, -jnp.inf))
    scores = jnp.einsum('bclgn,bcsgn->bclsg', cm, bm)
    y_diag = jnp.einsum('bclsg,bclsgr,bcsgrp->bclgrp', scores, decay, x)
    decay_to_end = jnp.exp(a_cum[:, :, -1:] - a_cum)
    chunk_states = jnp.einsum('bclgn,bclgr,bclgrp->bcgrpn', bm, decay_to_end, x)
    chunk_decay = jnp.exp(a_cum[:, :, -1])

    def step(state, inp):
        st, dec = inp
        return state * dec[..., None, None] + st, state

    init = jnp.zeros((b, g, r, p, n), chunk_states.dtype)
    _, states_in = lax.scan(step, init, (jnp.moveaxis(chunk_states, 1, 0), jnp.moveaxis(chunk_decay, 1, 0)))
    states_in = jnp.moveaxis(states_in, 0, 1)
    y_off = jnp.einsum('bclgn,bcgrpn,bclgr->bclgrp', cm, states_in, jnp.exp(a_cum))
    return (y_diag + y_off).reshape(b, s, h, p)

def mamba2_bidir(z, xbc, dt_f, dt_b, conv_w, conv_b, dt_bias_f, dt_bias_b, a_log_f, a_log_b, d_skip, norm_g):
    b, s, _ = z.shape
    xbc = jax.nn.silu(centred_depthwise_conv(xbc, conv_w, conv_b))
    xs, bm, cm = jnp.split(xbc, [SSM_D_INNER, SSM_D_INNER + SSM_GROUPS * SSM_STATE], axis=-1)
    xs = xs.reshape(b, s, SSM_HEADS, SSM_HEAD_DIM)
    bm = bm.reshape(b, s, SSM_GROUPS, SSM_STATE)
    cm = cm.reshape(b, s, SSM_GROUPS, SSM_STATE)

    def direction(xs_d, bm_d, cm_d, dt_raw, dt_bias, a_log):
        dt = jax.nn.softplus(dt_raw.astype(jnp.float32) + dt_bias.astype(jnp.float32))
        a = -jnp.exp(a_log.astype(jnp.float32)) * dt
        return ssd_scan(xs_d * dt[..., None], a, bm_d, cm_d, SSM_CHUNK)

    flip = lambda t: jnp.flip(t, axis=1)
    y_f = direction(xs, bm, cm, dt_f, dt_bias_f, a_log_f)
    y_b = flip(direction(flip(xs), flip(bm), flip(cm), flip(dt_b), dt_bias_b, a_log_b))
    y = y_f + y_b + d_skip.astype(jnp.float32)[:, None] * xs
    y = y.reshape(b, s, SSM_D_INNER) * jax.nn.silu(z.astype(jnp.float32))
    y = rms_norm(y.reshape(b, s, SSM_GROUPS, SSM_D_INNER // SSM_GROUPS),
                 norm_g.reshape(SSM_GROUPS, SSM_D_INNER // SSM_GROUPS))
    return y.reshape(b, s, SSM_D_INNER).astype(z.dtype)

def axial_rope_tables(seq):
    rows = seq // GRID_W
    row = jnp.repeat(jnp.arange(rows, dtype=jnp.float32), GRID_W)
    col = jnp.tile(jnp.arange(GRID_W, dtype=jnp.float32), rows)
    half = ATTN_HEAD_DIM // 2
    inv_freq = 1.0 / (ROPE_THETA ** (jnp.arange(0, half, 2, dtype=jnp.float32) / half))
    ang = jnp.concatenate([row[:, None] * inv_freq, col[:, None] * inv_freq], axis=-1)
    return jnp.cos(ang), jnp.sin(ang)

def apply_rope(x, cos, sin):
    b, s, h, d = x.shape
    xf = x.astype(jnp.float32).reshape(b, s, h, d // 2, 2)
    x0, x1 = xf[..., 0], xf[..., 1]
    c = cos[None, :, None, :]
    sn = sin[None, :, None, :]
    out = jnp.stack([x0 * c - x1 * sn, x0 * sn + x1 * c], axis=-1)
    return out.reshape(b, s, h, d).astype(x.dtype)

def gqa_bidir_blocks(q, k, v):
    b, s, hq, d = q.shape
    hkv = k.shape[2]
    r = hq // hkv
    nblk = s // ATTN_Q_BLOCK
    scale = d ** -0.5
    qb = (q * scale).reshape(b, nblk, ATTN_Q_BLOCK, hkv, r, d).transpose(1, 0, 2, 3, 4, 5)

    def one_block(qblk):
        sc = jnp.einsum('blkrd,bskd->bkrls', qblk, k).astype(jnp.float32)
        prob = jax.nn.softmax(sc, axis=-1).astype(v.dtype)
        return jnp.einsum('bkrls,bskd->blkrd', prob, v)

    out = lax.map(one_block, qb)
    return out.transpose(1, 0, 2, 3, 4, 5).reshape(b, s, hq * d)

def setup_inputs(seed: int = 0) -> dict:
    key = jax.random.key(seed)
    ks = jax.random.split(key, 24)
    f32 = jnp.float32
    nrm = lambda k, shape, scale: jax.random.normal(k, shape, f32) * scale
    gain = lambda k, shape: 1.0 + 0.02 * jax.random.normal(k, shape, f32)
    L = DEPTH
    dt_lo, dt_hi = 1e-3, 1e-1

    def dt_bias(k):
        u = jax.random.uniform(k, (L, SSM_HEADS), f32)
        dt = jnp.exp(u * (np.log(dt_hi) - np.log(dt_lo)) + np.log(dt_lo))
        return dt + jnp.log(-jnp.expm1(-dt))

    def a_log(k):
        return jnp.log(jax.random.uniform(k, (L, SSM_HEADS), f32, 1.0, 16.0))

    return {
        "x": jax.random.normal(ks[0], (BATCH, SEQ, D_MODEL), f32),
        "g_mix": gain(ks[1], (L, D_MODEL)),
        "w_in": nrm(ks[2], (L, D_MODEL, N_IN), D_MODEL ** -0.5),
        "conv_w": nrm(ks[3], (L, SSM_CONV_K, SSM_XBC), SSM_CONV_K ** -0.5),
        "conv_b": nrm(ks[4], (L, SSM_XBC), 0.02),
        "dt_bias_f": dt_bias(ks[5]),
        "dt_bias_b": dt_bias(ks[6]),
        "a_log_f": a_log(ks[7]),
        "a_log_b": a_log(ks[8]),
        "d_skip": gain(ks[9], (L, SSM_HEADS)),
        "ssm_norm_g": gain(ks[10], (L, SSM_D_INNER)),
        "q_norm_g": gain(ks[11], (L, ATTN_HEAD_DIM)),
        "k_norm_g": gain(ks[12], (L, ATTN_HEAD_DIM)),
        "w_ssm_up": nrm(ks[13], (L, SSM_D_INNER, D_MODEL), SSM_D_INNER ** -0.5),
        "w_attn_up": nrm(ks[14], (L, ATTN_Q_HEADS * ATTN_HEAD_DIM, D_MODEL), (ATTN_Q_HEADS * ATTN_HEAD_DIM) ** -0.5),
        "w_out": nrm(ks[15], (L, D_MODEL, D_MODEL), D_MODEL ** -0.5),
        "g_mlp": gain(ks[16], (L, D_MODEL)),
        "w_mlp_in": nrm(ks[17], (L, D_MODEL, D_FF), D_MODEL ** -0.5),
        "w_mlp_out": nrm(ks[18], (L, D_FF, D_MODEL), D_FF ** -0.5),
        "g_final": gain(ks[19], (D_MODEL,)),
    }

def reference(x, g_mix, w_in, conv_w, conv_b, dt_bias_f, dt_bias_b, a_log_f, a_log_b, d_skip,
              ssm_norm_g, q_norm_g, k_norm_g, w_ssm_up, w_attn_up, w_out, g_mlp, w_mlp_in,
              w_mlp_out, g_final):
    b, s, _ = x.shape
    cos, sin = axial_rope_tables(s)
    for layer in range(DEPTH):
        h = rms_norm(x, g_mix[layer])
        proj = h @ w_in[layer]
        z, xbc, dt_f, dt_b, q, k, v, gate_a, gate_b = jnp.split(proj, split_points(IN_SIZES), axis=-1)

        y_ssm = mamba2_bidir(z, xbc, dt_f, dt_b, conv_w[layer], conv_b[layer],
                             dt_bias_f[layer], dt_bias_b[layer], a_log_f[layer], a_log_b[layer],
                             d_skip[layer], ssm_norm_g[layer])

        q = rms_norm(q.reshape(b, s, ATTN_Q_HEADS, ATTN_HEAD_DIM), q_norm_g[layer])
        k = rms_norm(k.reshape(b, s, ATTN_KV_HEADS, ATTN_HEAD_DIM), k_norm_g[layer])
        v = v.reshape(b, s, ATTN_KV_HEADS, ATTN_HEAD_DIM)
        q = apply_rope(q, cos, sin)
        k = apply_rope(k, cos, sin)
        y_attn = gqa_bidir_blocks(q, k, v)

        branch_a = y_ssm @ w_ssm_up[layer]
        branch_b = y_attn @ w_attn_up[layer]
        merged = jax.nn.sigmoid(gate_a) * branch_a + jax.nn.sigmoid(gate_b) * branch_b
        x = x + merged @ w_out[layer]
        h2 = rms_norm(x, g_mlp[layer])
        x = x + jnp.square(jax.nn.relu(h2 @ w_mlp_in[layer])) @ w_mlp_out[layer]
    return rms_norm(x, g_final)


_drawn_inputs = setup_inputs


def setup_inputs(seed=0):
    import zlib

    import numpy as np

    out = dict(_drawn_inputs(seed))
    spreads = {}
    factors = {'g_mix': 3.369,
     'conv_b': 3.547,
     'd_skip': 200.0,
     'ssm_norm_g': 16.533,
     'q_norm_g': 8.0,
     'k_norm_g': 8.0,
     'g_mlp': 10.739,
     'g_final': 24.805}
    for name, (base, spread) in spreads.items():
        noise = np.random.default_rng([zlib.crc32(name.encode()), seed]).standard_normal(out[name].shape)
        drawn = base * np.exp(spread * noise) if base else spread * noise
        out[name] = __import__('jax').numpy.asarray(drawn.astype(out[name].dtype))
    for name, factor in factors.items():
        out[name] = (out[name] * factor).astype(out[name].dtype)
    return out
```

```python
from contextlib import ExitStack

import concourse.bass as bass
import numpy as np
from concourse import mybir

ALU = mybir.AluOpType
ACT = mybir.ActivationFunctionType
AX_X = mybir.AxisListType.X
F32 = mybir.dt.float32
F32R = mybir.dt.float32r
ds = bass.ds

P = 128
D = 2048
T = 256
TB = T // P
KT = D // P
N = 512
PIECES = 8
RING = 4
LEAD = 2
HEADS = 32
HD = 64
GROUPS = 8
TAPS = 5
QH, KVH, AD = 16, 4, 128
D_FF = 4 * D
EPS = 1e-6
SCALE = float(AD) ** -0.5
COL_Z = 0
COL_XS = COL_Z + D
COL_B = COL_XS + D
COL_C = COL_B + GROUPS * P
COL_DT = COL_C + GROUPS * P
COL_Q = COL_DT + 2 * HEADS
COL_K = COL_Q + QH * AD
COL_V = COL_K + KVH * AD
COL_GA = COL_V + KVH * AD
COL_GB = COL_GA + D
DTW = 2 * HEADS
assert KT * DTW <= 2 * N

U_XBC, U_Z, U_K, U_V, U_Q, U_GATE, U_OUT, U_MLP = 0, 8, 12, 13, 14, 18, 34, 38
U_END = U_MLP + 32
TS_X, TS_Z, TS_MERGED, TS_X2, TS_HID = 0, 4, 8, 12, 16
THREES = 9


def walk(eng, window):
    window(0, 0, "xbc", 0, [("rates", 0)])
    window(0, 1, "xbc", 1, [("conv", 0), ("decays", 0)])
    window(1, 0, "xbc", 2, [("conv", 1), ("scan", 0)])
    window(1, 1, "xbc", 3, [("conv", 2), ("scan", 1)])
    with eng.Fori(1, 3) as i:
        window(i + 1, 0, "xbc", 2 * i + 2, [("conv", 2 * i + 1), ("scan", 2 * i)])
        window(i + 1, 1, "xbc", 2 * i + 3, [("conv", 2 * i + 2), ("scan", 2 * i + 1)])
    window(4, 0, "z", 0, [("conv", 7), ("scan", 6)])
    window(4, 1, "z", 1, [("zgate", 0), ("scan", 7)])
    window(5, 0, "z", 2, [("zgate", 1)])
    window(5, 1, "z", 3, [("zgate", 2)])
    window(6, 0, "k", 0, [("zgate", 3)])
    window(6, 1, "v", 0, [("rope", 0)])
    window(7, 0, "q", 0, [("values", 0)])
    window(7, 1, "q", 1, [("rope", 1)])
    window(8, 0, "q", 2, [("attend", 0), ("rope", 2)])
    window(8, 1, "q", 3, [("attend", 1), ("rope", 3)])
    window(9, 0, "ga", 0, [("attend", 2), ("rope", 4)])
    window(9, 1, "gb", 0, [("attend", 3), ("gate_a", 0)])
    with eng.Fori(0, 3) as j:
        window(2 * j + 10, 0, "ssm_up", j, [("gate_b", j)])
        window(2 * j + 10, 1, "attn_up", j, [("gated_a", j)])
        window(2 * j + 11, 0, "ga", j + 1, [("merged", j)])
        window(2 * j + 11, 1, "gb", j + 1, [("gate_a", j + 1)])
    window(16, 0, "ssm_up", 3, [("gate_b", 3)])
    window(16, 1, "attn_up", 3, [("gated_a", 3)])
    window(17, 0, "out", 0, [("merged", 3)])
    window(17, 1, "out", 1, [("residual", 0)])
    window(18, 0, "out", 2, [("residual", 1)])
    window(18, 1, "out", 3, [("residual", 2)])
    window(19, 0, "mlp_in", (0, 0), [("residual", 3)])

    def rest_of_hidden_group(g):
        for j in range(1, 4):
            window(4 * g + 19 + j // 2, j % 2, "mlp_in", (g, j), [("hidden", (g, j - 1))])
        window(4 * g + 21, 0, "mlp_out", (g, 0), [("hidden", (g, 3))])
        for j in range(1, 4):
            window(4 * g + 21 + j // 2, j % 2, "mlp_out", (g, j), [("add", j - 1)])

    with eng.Fori(0, 3) as g:
        rest_of_hidden_group(g)
        window(4 * g + 23, 0, "mlp_in", (g + 1, 0), [("add", 3)])
    rest_of_hidden_group(3)


def piece_number(r, par, p):
    return r * (2 * PIECES) + (1 + PIECES * par + p)


def landed_count(r, par, p, threes):
    uses = r * (2 * PIECES // RING) + (PIECES // RING * par + p // RING + 1)
    extra = 16 if p % RING == RING - 1 else 0
    if threes:
        return uses * 48 + extra
    return uses * 16 + (extra + 32 * THREES * PIECES // RING)


def previous(r, par):
    return (r, 0) if par else (r - 1, 1)


def first(idx):
    return isinstance(idx, int) and idx == 0


def build(nc, x, g_mix, w_in, conv_w, conv_b, dt_bias_f, dt_bias_b, a_log_f, a_log_b, d_skip,
          ssm_norm_g, q_norm_g, k_norm_g, w_ssm_up, w_attn_up, w_out, g_mlp, w_mlp_in, w_mlp_out,
          g_final, consts, out):
    top = [-(-nc.sbuf_base // 64) * 64]

    def place(name, shape, dt=F32):
        n = 4
        for s in shape[1:]:
            n *= s
        t = nc.alloc_sbuf_tensor_at(name, shape, dt, offset=top[0])
        top[0] += -(-n // 32) * 32
        return t

    raw = place("raw", [P, RING, 2 * N])
    whi = place("whi", [P, RING, 2 * N], F32R)
    wlo = place("wlo", [P, RING, 2 * N], F32R)
    a_hi = place("a_hi", [P, KT, T], F32R)
    a_lo = place("a_lo", [P, KT, T], F32R)
    x_sb = place("x_sb", [P, TB, D])
    tmp_a = place("tmp_a", [P, TB, N])
    tmp_b = place("tmp_b", [P, TB, N])
    ident = place("ident", [P, P])
    gains = place("gains", [P, 3 * KT])
    rope_t = place("rope_t", [P, 2, 2, TB, AD])
    rstd = place("rstd", [P, TB])
    half_rstd = place("half_rstd", [P, TB])
    rstd_mlp = place("rstd_mlp", [P, TB])
    rstd_out = place("rstd_out", [P, TB])
    x_ss = place("x_ss", [P, TB])
    x_var = place("x_var", [P, TB])
    rows_ss = place("rows_ss", [P, TB, 4])
    z_ss = place("z_ss", [P, 4])
    z_rs = place("z_rs", [P, 4])
    q_ss = place("q_ss", [P, TB, 4])
    q_rs = place("q_rs", [P, TB, 4])
    minus_half = place("minus_half", [P, 8])

    region_b = top[0]
    xt = place("xt", [P, TB * N])
    cv = place("cv", [P, 4, T + TAPS - 1])
    acc = place("acc", [P, 4, T])
    cw = place("cw", [P, GROUPS, 4, TAPS + 1])
    param_rows = place("param_rows", [3 * 2 * KT, 3, P])
    rope_raw = place("rope_raw", [P, 2, TB, AD])
    qk_gain = place("qk_gain", [P, 2, AD])
    end_b = top[0]
    top[0] = region_b
    b_hi = place("b_hi", [P, KT, T], F32R)
    b_lo = place("b_lo", [P, KT, T], F32R)
    assert end_b <= top[0]

    region_y = top[0]
    y_sb = place("y_sb", [P, TB, D])
    end_y = top[0]
    top[0] = region_y
    kT = place("kT", [P, KVH, T])
    v_sb = place("v_sb", [P, TB, KVH, AD])
    prob = place("prob", [P, 4, TB, T])
    assert top[0] <= end_y
    top[0] = region_y
    m_hi = place("m_hi", [P, KT, T], F32R)
    assert top[0] <= end_y
    top[0] = end_y

    region_r = top[0]
    masks = place("masks", [P, 4, P])
    cs = place("cs", [P, 4, T])
    tm = place("tm", [P, TB, 3 * P])
    masks_r = place("masks_r", [P, 2, P], F32R)
    mv_hi = place("mv_hi", [P, TB, 2, 4, P], F32R)
    mv_lo = place("mv_lo", [P, TB, 2, 4, P], F32R)
    ex = place("ex", [P, TB, 4, P])
    mw = place("mw", [P, 2, TB, 4, P])
    mw_b = tmp_b[:, 0, :].rearrange("p (h l) -> p h l", h=4)
    xd = place("xd", [P, TB, 4, HD])
    st = place("st", [P, TB, 4 * HD])
    t1 = place("t1", [P, TB, 4, HD])
    t2 = place("t2", [P, TB, 4, HD])
    dt_bias = place("dt_bias", [P, 2, HEADS])
    exp_a = place("exp_a", [P, 2, HEADS])
    dskip = place("dskip", [P, HEADS])
    dtv = place("dtv", [P, TB, 2, HEADS])
    av = place("av", [P, TB, 2, HEADS])
    av_hi = place("av_hi", [P, TB, 2, HEADS], F32R)
    av_lo = place("av_lo", [P, TB, 2, HEADS], F32R)
    dec = place("dec", [P, 4, HEADS])
    wdt = place("wdt", [P, TB, HEADS])
    assert top[0] <= nc.sbuf_usable_end, (top[0], nc.sbuf_usable_end)
    top[0] = region_r
    c_hi = place("c_hi", [P, KT, T], F32R)
    c_lo = place("c_lo", [P, KT, T], F32R)
    region_r2 = top[0]
    qT = place("qT", [P, 4, T])
    pT = place("pT", [P, 2, TB, T])
    vg = place("vg", [P, TB, AD])
    mx = place("mx", [P, 4, TB])
    nb = place("nb", [P, 4, TB])
    den = place("den", [P, 4, TB])
    rden = place("rden", [P, 4, TB])
    top[0] = region_r2
    m_lo = place("m_lo", [P, KT, T], F32R)
    assert top[0] <= nc.sbuf_usable_end, (top[0], nc.sbuf_usable_end)
    top[0] = region_r
    g_last = place("g_last", [P, D])
    fin = place("fin", [P, TB, D])

    keep = ExitStack()

    def sem(name):
        return keep.enter_context(nc.semaphore(name))

    G = keep.enter_context(nc.psum_tensor("G", [P, 4, N], F32))
    S = keep.enter_context(nc.psum_tensor("S", [P, 4, N], F32))

    s_ident, s_gains, s_taps, s_masks, s_rope, s_dt_in = [
        sem(f"s_{n}") for n in ("ident", "gains", "taps", "masks", "rope", "dt_in")]
    s_x = [sem(f"s_x{c}") for c in range(4)]
    s_g_last, s_store = sem("s_g_last"), sem("s_store")
    landed = [sem(f"landed{i}") for i in range(RING)]
    hi_made = sem("hi_made")
    lo_made = sem("lo_made")
    used = sem("used")
    taken = [sem("taken0"), sem("taken1")]
    rows_t = sem("rows_t")
    set_up = sem("set_up")
    set_cv = sem("set_cv")
    expo = sem("expo")
    ts_t, ts_hi, ts_lo = sem("ts_t"), sem("ts_hi"), sem("ts_lo")
    sq_x, var_x, rstd_x = sem("sq_x"), sem("var_x"), sem("rstd_x")
    dt_v, dt_e, dt_mm, dt_dec = sem("dt_v"), sem("dt_e"), sem("dt_mm"), sem("dt_dec")
    conv_t, cv_made, conv_v, th_made = sem("conv_t"), sem("cv_made"), sem("conv_v"), sem("th_made")
    back_t, tm_made, score_mm, scan_v = sem("back_t"), sem("tm_made"), sem("score_mm"), sem("scan_v")
    mv_made, t2_made, seg_mm, ex_made = sem("mv_made"), sem("t2_made"), sem("seg_mm"), sem("ex_made")
    mw_made, mw_steps, dt_t, masks_made = sem("mw_made"), sem("mw_steps"), sem("dt_t"), sem("masks_made")
    st_mm, st_made, y_mm, off_mm = sem("st_mm"), sem("st_made"), sem("y_mm"), sem("off_mm")
    z_v, z_sq, z_root = sem("z_v"), sem("z_sq"), sem("z_root")
    r_sq, r_v, r_root, r_t, r_made = sem("r_sq"), sem("r_v"), sem("r_root"), sem("r_t"), sem("r_made")
    vg_made, at_sc, at_max, at_exp = sem("vg_made"), sem("at_sc"), sem("at_max"), sem("at_exp")
    at_v, at_t, at_pt, at_pv = sem("at_v"), sem("at_t"), sem("at_pt"), sem("at_pv")
    at_hi, at_lo = sem("at_hi"), sem("at_lo")
    merge_v, hid_sq, fin_v = sem("merge_v"), sem("hid_sq"), sem("fin_v")

    CONV_V = 4 * TAPS + 1
    SCAN_V = 9
    Z_V = 7
    ROPE_V = 11
    AT_V = 3
    DT_A = 22

    def product(par, tb):
        return G[:, 2 * par + tb, :]

    def x_bank(j, c, part=slice(0, T)):
        bank = (G[:, 0:2, :], G[:, 2:4, :], S[:, 0:2, :])[j % 3]
        return bank[:, c // 2, c % 2 * T + part.start:c % 2 * T + part.stop]

    u_dt = tmp_a[:, :, :].rearrange("p b n -> p (b n)")[:, 0:6 * TB * DTW].rearrange(
        "p (m n) -> p m n", m=6)
    dt_rows = u_dt[0:DTW, 3:5, :].rearrange("p a b -> p (a b)")

    def done(r, par):
        return piece_number(r, par, PIECES)

    block = keep.enter_context(nc.Block())

    @block.sync
    def _(sp):
        w_in_k = w_in.rearrange("a (k p) n -> (a p) k n", p=P)
        mats = {"ssm_up": w_ssm_up, "attn_up": w_attn_up, "out": w_out, "mlp_in": w_mlp_in,
                "mlp_out": w_mlp_out}
        mats = {n: w.rearrange("a (k p) n -> (a p) k n", p=P) for n, w in mats.items()}
        cols = {"z": COL_Z, "k": COL_K, "v": COL_V, "q": COL_Q, "ga": COL_GA, "gb": COL_GB}

        x_k = x.rearrange("a (b p) n -> (a p) b n", p=P)
        for c in range(4):
            sp.dma_start(x_sb[:, :, c * N:(c + 1) * N], x_k[:, :, c * N:(c + 1) * N]).then_inc(s_x[c], 16)
        sp.dma_start(raw[:, RING - 1, 0:KT * DTW].rearrange("p (k n) -> p k n", k=KT),
                     w_in_k[:, :, COL_DT:COL_DT + DTW]).then_inc(landed[RING - 1], 16)

        def window(r, par, kind, idx, sides):
            for p in range(PIECES):
                dst = raw[:, p % RING, :].rearrange("p (k n) -> p k n", k=2)
                if not (isinstance(r, int) and piece_number(r, par, p) < RING):
                    sp.wait_ge(lo_made, piece_number(r, par, p) - RING + 1)
                if kind == "xbc" or (kind == "z" and idx == 0):
                    if kind == "xbc":
                        at, pair, step = idx * (2 * P) + COL_XS, idx * P + COL_B, COL_C - COL_B
                    else:
                        at, pair, step = COL_Z, COL_Z + 2 * P, P
                    sp.dma_start(dst[:, :, 0:2 * P], w_in_k[:, 2 * p:2 * p + 2, ds(at, 2 * P)]
                                 ).then_inc(landed[p % RING], 16)
                    for t in range(2):
                        sp.dma_start(dst[:, :, (2 + t) * P:(3 + t) * P],
                                     w_in_k[:, 2 * p:2 * p + 2, ds(pair + t * step, P)]
                                     ).then_inc(landed[p % RING], 16)
                    continue
                if kind == "mlp_in":
                    src = mats[kind][:, 2 * p:2 * p + 2, ds((idx[0] * 4 + idx[1]) * N, N)]
                elif kind == "mlp_out":
                    src = mats[kind][:, ds(idx[0] * KT + 2 * p, 2), idx[1] * N:(idx[1] + 1) * N]
                elif kind in mats:
                    src = mats[kind][:, 2 * p:2 * p + 2, ds(idx * N, N)]
                else:
                    src = w_in_k[:, 2 * p:2 * p + 2, ds(idx * N + cols[kind], N)]
                sp.dma_start(dst, src).then_inc(landed[p % RING], 16)

        walk(sp, window)
        sp.wait_ge(used, done(16, 1))
        sp.dma_start(g_last[:, :], g_final.rearrange("(a n) -> a n", a=1).to_broadcast([P, D])
                     ).then_inc(s_g_last, 16)
        o_k = out.rearrange("a (b p) n -> (a p) b n", p=P)
        for tb in range(TB):
            sp.wait_ge(fin_v, tb + 1)
            sp.dma_start(o_k[:, tb, :], fin[:, tb, :]).then_inc(s_store, 16)
        sp.wait_ge(s_store, 16 * TB)

    @block.scalar
    def _(act):
        act.dma_start(ident[:, :], consts[:, 0:P]).then_inc(s_ident, 16)
        for n, g in enumerate((g_mix, g_mlp, ssm_norm_g)):
            act.dma_start(param_rows[n * KT:(n + 1) * KT, 0, :],
                          g.rearrange("a (k p) -> (a k) p", p=P)).then_inc(s_gains, 16)
        taps = conv_w.rearrange("a t (k p) -> (a t k) p", p=P)
        rows = 2 * KT
        act.dma_start(param_rows[:, 1, :], taps[0:3 * rows, :]).then_inc(s_taps, 16)
        act.dma_start(param_rows[0:2 * rows, 2, :], taps[3 * rows:5 * rows, :]).then_inc(s_taps, 16)
        act.dma_start(param_rows[2 * rows:3 * rows, 2, :],
                      conv_b.rearrange("a (k p) -> (a k) p", p=P)).then_inc(s_taps, 16)
        for n, (b, a) in enumerate(((dt_bias_f, a_log_f), (dt_bias_b, a_log_b))):
            act.dma_start(dt_bias[:, n, :], b.to_broadcast([P, HEADS])).then_inc(s_dt_in, 16)
            act.dma_start(exp_a[:, n, :], a.to_broadcast([P, HEADS])).then_inc(s_dt_in, 16)
        act.dma_start(dskip[:, :], d_skip.to_broadcast([P, HEADS])).then_inc(s_dt_in, 16)
        act.dma_start(masks[:, :, :].rearrange("p m n -> p (m n)"), consts[:, P:5 * P]).then_inc(s_masks, 16)
        act.dma_start(rope_raw[:, :, :, :].rearrange("p a b n -> p (a b n)"),
                      consts[:, 5 * P:9 * P]).then_inc(s_rope, 16)
        for n, g in enumerate((q_norm_g, k_norm_g)):
            act.dma_start(qk_gain[:, n, :], g.to_broadcast([P, AD])).then_inc(s_rope, 16)

        def split(n, slot, width, arrived):
            act.wait_ge(landed[slot], arrived)
            if not isinstance(n, int) or n >= RING:
                act.wait_ge(used, n - RING + 1)
            act.activation(whi[:, slot, 0:width], raw[:, slot, 0:width], ACT.Copy).then_inc(hi_made, 1)

        def split_high(rnd, dst, k0, gain=None, factor=1.0):
            act.wait_ge(ts_t, rnd + 1)
            if gain is None:
                for c in range(2):
                    last = act.activation(dst[:, ds(k0 + 2 * c, 2), :],
                                          S[:, c, :].rearrange("p (c t) -> p c t", c=2), ACT.Copy,
                                          scale=factor)
            else:
                for c in range(4):
                    last = act.activation(dst[:, k0 + c, :], S[:, c // 2, c % 2 * T:(c % 2 + 1) * T],
                                          ACT.Copy, scale=gains[:, gain * KT + k0 + c:gain * KT + k0 + c + 1])
            last.then_inc(ts_hi, 1)

        act.wait_ge(set_up, 1)
        for j in range(4):
            act.wait_ge(ts_t, TS_X + j + 1)
            for c in range(4):
                k = 4 * j + c
                last = act.activation(a_hi[:, k, :], x_bank(j, c), ACT.Copy, scale=gains[:, k:k + 1])
            last.then_inc(ts_hi, 1)
            if j == 0:
                split(0, RING - 1, KT * DTW, 16)
        for p in range(LEAD):
            split(piece_number(0, 0, p), p, 2 * N, landed_count(0, 0, p, True))

        def rates(p, _, pr, pp):
            if p == 0:
                act.wait_ge(used, 1)
                act.activation(dt_rows, S[0:DTW, 2, 0:T], ACT.Copy).then_inc(dt_e, 1)
            if p in (1, 2):
                act.activation(y_sb[:, p - 1, :], x_sb[:, p - 1, :], ACT.Square,
                               accum_out=x_ss[:, p - 1:p]).then_inc(sq_x, 1)
            if p == 3:
                act.wait_ge(s_dt_in, 16 * 5)
                act.activation(exp_a[:, :, :], exp_a[:, :, :], ACT.Exp).then_inc(dt_e, 1)
                act.wait_ge(s_masks, 16)
                act.activation(masks_r[:, :, :], masks[:, 0:2, :], ACT.Copy).then_inc(masks_made, 1)
            if p == 5:
                act.wait_ge(dt_v, 4)
                act.activation(u_dt[:, 2, :], u_dt[:, 1, :], ACT.Exp).then_inc(dt_e, 1)

        def decays(p, _, pr, pp):
            if p == 1:
                act.wait_ge(dt_mm, 1)
                act.activation(dec[:, :, :].rearrange("p a b -> p (a b)"), S[:, 3, 0:4 * HEADS], ACT.Exp
                               ).then_inc(dt_dec, 1)

        def conv(p, g, pr, pp):
            if p == 0:
                act.wait_ge(used, done(pr, pp))
                act.wait_ge(rstd_x, 1)
                if not first(g):
                    act.wait_ge(conv_v, g * CONV_V)
                for tb in range(TB):
                    last = act.activation(xt[:, tb * N:(tb + 1) * N], product(pp, tb), ACT.Copy,
                                          scale=rstd[:, tb:tb + 1])
                last.then_inc(taken[pp], 1)
            if p == 2:
                act.wait_ge(conv_t, g + 1)
                for c in range(2):
                    act.activation(cv[:, 2 * c:2 * c + 2, TAPS // 2:TAPS // 2 + T],
                                   S[:, c, :].rearrange("p (c t) -> p c t", c=2), ACT.Copy
                                   ).then_inc(cv_made, 1)
            if p == 6:
                act.wait_ge(conv_v, g * CONV_V + (CONV_V - 1))
                act.activation(xt[:, :], acc[:, :, :].rearrange("p c t -> p (c t)"), ACT.Tanh
                               ).then_inc(th_made, 1)

        def scan(p, g, pr, pp):
            if p == 0:
                act.wait_ge(back_t, g + 1)
                if not first(g):
                    act.wait_ge(scan_v, g * SCAN_V)
                    act.wait_ge(t2_made, 2 * g)
                    act.wait_ge(y_mm, 2 * g)
                for tb in range(TB):
                    act.activation(tm[:, tb, :], S[:, 1 + 2 * tb, 0:3 * P], ACT.Copy).then_inc(tm_made, 1)
            if p in (2, 3):
                c = p - 2
                act.wait_ge(seg_mm, 2 * g + (c + 1))
                if not first(g):
                    act.wait_ge(scan_v, g * SCAN_V)
                act.activation(ex[:, c, :, :].rearrange("p h l -> p (h l)"), S[:, 2 + c, :], ACT.Exp
                               ).then_inc(ex_made, 1)
            if p == 4:
                act.wait_ge(st_mm, g + 1)
                if not first(g):
                    act.wait_ge(off_mm, g)
                act.activation(st[:, :, :].rearrange("p a b -> p (a b)"), S[:, 3, :], ACT.Copy
                               ).then_inc(st_made, 1)

        def zgate(p, j, pr, pp):
            if p == 0:
                act.wait_ge(used, done(pr, pp))
                act.wait_ge(ts_t, TS_Z + j)
                if j == 0:
                    act.wait_ge(mw_made, TB * GROUPS)
                for tb in range(TB):
                    act.activation(tmp_a[:, tb, :], product(pp, tb), ACT.Copy, scale=rstd[:, tb:tb + 1])
                for tb in range(TB):
                    last = act.activation(tmp_b[:, tb, :], product(pp, tb), ACT.Tanh,
                                          scale=half_rstd[:, tb:tb + 1])
                last.then_inc(taken[pp], 1)
            if p == 2:
                act.wait_ge(z_v, j * Z_V + 2)
                for tb in range(TB):
                    for gg in range(2):
                        act.activation(tmp_b[:, tb, gg * T:(gg + 1) * T], tmp_a[:, tb, gg * T:(gg + 1) * T],
                                       ACT.Square, scale=0.5,
                                       accum_out=z_ss[:, 2 * tb + gg:2 * tb + gg + 1]).then_inc(z_sq, 1)
            if p == 7:
                split_high(TS_Z + j, b_hi, 4 * j, gain=2)

        def rope(p, n, pr, pp):
            if p == 0:
                act.wait_ge(used, done(pr, pp))
                if not first(n):
                    act.wait_ge(r_v, n * ROPE_V)
                for tb in range(TB):
                    act.activation(tmp_b[:, tb, :], product(pp, tb), ACT.Square, scale=rstd[:, tb:tb + 1]
                                   ).then_inc(r_sq, 1)
            if p == 2:
                act.wait_ge(r_root, 2 * (n + 1))
                if first(n):
                    act.wait_ge(ts_t, TS_MERGED)
                else:
                    act.wait_ge(r_t, n)
                for tb in range(TB):
                    for h in range(4):
                        last = act.activation(tmp_a[:, tb, h * AD:(h + 1) * AD],
                                              product(pp, tb)[:, h * AD:(h + 1) * AD], ACT.Copy,
                                              scale=q_rs[:, tb, h:h + 1])
                last.then_inc(taken[pp], 1)
            if p == 7:
                act.wait_ge(r_t, n + 1)
                if n >= 2:
                    act.wait_ge(at_sc, 4 * (n - 1))
                dst = qT if n else kT
                for c in range(2):
                    act.activation(dst[:, 2 * c:2 * c + 2, :], S[:, c, :].rearrange("p (c t) -> p c t", c=2),
                                   ACT.Copy).then_inc(r_made, 1)

        def values(p, n, pr, pp):
            if p == 0:
                act.wait_ge(used, done(pr, pp))
                for tb in range(TB):
                    last = act.activation(v_sb[:, tb, :, :].rearrange("p h d -> p (h d)"), product(pp, tb),
                                          ACT.Copy, scale=rstd[:, tb:tb + 1])
                last.then_inc(taken[pp], 1)

        def attend(p, g, pr, pp):
            def exps(h):
                act.wait_ge(at_max, 8 * g + 2 * h + 2)
                if g:
                    act.wait_ge(at_t, 4 * (g - 1) + h + 1)
                for tb in range(TB):
                    act.activation(prob[:, h, tb, :], S[:, h % 2, tb * T:(tb + 1) * T], ACT.Exp,
                                   bias=nb[:, h, tb:tb + 1], scale=SCALE,
                                   accum_out=den[:, h, tb:tb + 1]).then_inc(at_exp, 1)

            def copy_pt(h):
                act.wait_ge(at_t, 4 * g + h + 1)
                if 4 * g + h >= 2:
                    act.wait_ge(at_pv, 4 * g + h - 1)
                act.activation(pT[:, h % 2, :, :].rearrange("p s l -> p (s l)"), S[:, 2, :], ACT.Copy
                               ).then_inc(at_pt, 1)

            def high(pair):
                act.wait_ge(at_pv, 4 * g + 2 * pair + 2)
                act.activation(c_hi[:, 4 * g + 2 * pair:4 * g + 2 * pair + 2, :],
                               S[:, 3, :].rearrange("p (c t) -> p c t", c=2), ACT.Copy).then_inc(at_hi, 1)

            if p in (0, 1):
                exps(2 * p)
                exps(2 * p + 1)
            if 2 <= p <= 5:
                copy_pt(p - 2)
            if p == 5:
                high(0)
            if p == 7:
                high(1)

        def gate(dst, pr, pp):
            act.wait_ge(used, done(pr, pp))
            for tb in range(TB):
                last = act.activation(dst[:, tb, :], product(pp, tb), ACT.Tanh, scale=half_rstd[:, tb:tb + 1])
            last.then_inc(taken[pp], 1)

        def gate_a(p, j, pr, pp):
            if p == 0:
                if first(j):
                    act.wait_ge(r_t, 5)
                else:
                    act.wait_ge(merge_v, j)
                gate(tmp_a, pr, pp)

        def gate_b(p, j, pr, pp):
            if p == 0:
                act.wait_ge(ts_t, j + TS_MERGED)
                gate(tmp_b, pr, pp)

        def merged(p, j, pr, pp):
            if p == 2:
                split_high(j + TS_MERGED, m_hi, j * 4, factor=0.5)

        def residual(p, j, pr, pp):
            if p == 2:
                split_high(TS_X2 + j, b_hi, 4 * j, gain=1)
                for tb in range(TB):
                    act.activation(tmp_a[:, tb, :], x_sb[:, tb, j * N:(j + 1) * N], ACT.Square,
                                   accum_out=rows_ss[:, tb, j:j + 1]).then_inc(sq_x, 1)

        def hidden(p, idx, pr, pp):
            g, j = idx
            if p == 0:
                act.wait_ge(used, done(pr, pp))
                act.wait_ge(rstd_x, 2)
                for tb in range(TB):
                    last = act.activation(tmp_a[:, tb, :], product(pp, tb), ACT.Relu,
                                          scale=rstd_mlp[:, tb:tb + 1])
                last.then_inc(taken[pp], 1)
                act.wait_ge(ts_t, g * 4 + (TS_HID + j))
                act.wait_ge(taken[pp], pr + 1)
                act.activation(tmp_b[:, :, :], tmp_a[:, :, :], ACT.Square).then_inc(hid_sq, 1)
            if p == 2:
                split_high(g * 4 + (TS_HID + j), a_hi, 4 * j)

        table = {f.__name__: f for f in (rates, decays, conv, scan, zgate, rope, values, attend, gate_a, gate_b,
                                         merged, residual, hidden)}

        def window(r, par, kind, idx, sides):
            for p in range(PIECES):
                q = p + LEAD
                if not (isinstance(r, int) and 2 * r + par == U_END - 1 and q >= PIECES):
                    threes = kind == "xbc" or (kind == "z" and idx == 0 and q < PIECES)
                    split(piece_number(r, par, q), q % RING, 2 * N, landed_count(r, par, q, threes))
                for name, at in sides:
                    if name in table:
                        table[name](p, at, *previous(r, par))

        walk(act, window)
        act.wait_ge(taken[1], U_END // 2)
        for tb in range(TB):
            act.activation(y_sb[:, tb, :], x_sb[:, tb, :], ACT.Square, accum_out=x_ss[:, tb:tb + 1]
                           ).then_inc(sq_x, 1)

    @block.vector
    def _(dve):
        def split(n, slot, width):
            dve.wait_ge(hi_made, n + 1)
            dve.tensor_tensor(wlo[:, slot, 0:width], raw[:, slot, 0:width],
                              whi[:, slot, 0:width].bitcast(F32), ALU.subtract).then_inc(lo_made, 1)

        def split_low(rnd, hi, lo, k0, gain=None, factor=1.0):
            dve.wait_ge(ts_hi, rnd + 1)
            if gain is None:
                for c in range(2):
                    last = dve.scalar_tensor_tensor(
                        out=lo[:, ds(k0 + 2 * c, 2), :], in0=S[:, c, :].rearrange("p (c t) -> p c t", c=2),
                        scalar=factor, in1=hi[:, ds(k0 + 2 * c, 2), :].bitcast(F32),
                        op0=ALU.mult, op1=ALU.subtract)
            else:
                for c in range(4):
                    k = gain * KT + k0 + c
                    last = dve.scalar_tensor_tensor(
                        out=lo[:, k0 + c, :], in0=S[:, c // 2, c % 2 * T:(c % 2 + 1) * T],
                        scalar=gains[:, k:k + 1], in1=hi[:, k0 + c, :].bitcast(F32),
                        op0=ALU.mult, op1=ALU.subtract)
            last.then_inc(ts_lo, 1)

        half = TAPS // 2
        dve.memset(cv[:, :, 0:half], 0.0).then_inc(set_cv, 1)
        dve.memset(cv[:, :, half + T:2 * half + T], 0.0).then_inc(set_cv, 1)
        dve.wait_ge(rows_t, 1)
        dve.tensor_copy(gains[:, :], S[:, 3, 0:3 * KT]).then_inc(set_up, 1)
        dve.wait_ge(set_up, 1)
        for j in range(4):
            dve.wait_ge(ts_hi, TS_X + j + 1)
            for c in range(4):
                k = 4 * j + c
                last = dve.scalar_tensor_tensor(
                    out=a_lo[:, k, :], in0=x_bank(j, c), scalar=gains[:, k:k + 1],
                    in1=a_hi[:, k, :].bitcast(F32), op0=ALU.mult, op1=ALU.subtract)
            last.then_inc(ts_lo, 1)
            if j == 0:
                split(0, RING - 1, KT * DTW)
        for p in range(LEAD):
            split(piece_number(0, 0, p), p, 2 * N)

        def pairs(t):
            return t.rearrange("p (i two) -> p i two", two=2)

        def rates(p, _, pr, pp):
            if p == 0:
                dve.wait_ge(rows_t, 2)
                weights = S[:, 3, 3 * KT:3 * KT + 6 * 2 * KT].rearrange("p (t k) -> p t k", t=TAPS + 1)
                for c in range(4):
                    tiles = weights[:, :, c:2 * GROUPS:2] if c < 2 else weights[:, :, c * GROUPS:(c + 1) * GROUPS]
                    dve.tensor_scalar(cw[:, :, c, :].rearrange("p g t -> p t g"), tiles, 0.5, None, ALU.mult
                                      ).then_inc(set_up, 1)
            if p == 3:
                dve.wait_ge(s_rope, 16 * 3)
                for n in range(2):
                    gain = qk_gain[:, n, :]
                    dve.tensor_tensor(rope_t[:, n, 0, :, :], rope_raw[:, 0, :, :],
                                      gain.unsqueeze(1).to_broadcast([P, TB, AD]), ALU.mult
                                      ).then_inc(set_up, 1)
                    for e in range(2):
                        dve.tensor_tensor(
                            rope_t[:, n, 1, :, e:AD:2], rope_raw[:, 1, :, e:AD:2],
                            gain[:, 1 - e:AD:2].unsqueeze(1).to_broadcast([P, TB, AD // 2]), ALU.mult
                        ).then_inc(set_up, 1)
            if p == 2:
                dve.wait_ge(sq_x, TB)
                dve.tensor_scalar(x_var[:, :], x_ss[:, :], 1.0 / D, EPS, ALU.mult, ALU.add).then_inc(var_x, 1)
            if p == 4:
                dve.wait_ge(rstd_x, 1)
                dve.tensor_scalar(half_rstd[:, :], rstd[:, :], 0.5, None, ALU.mult).then_inc(var_x, 1)
                dve.wait_ge(s_dt_in, 16 * 5)
                dve.wait_ge(dt_t, 1)
                u, m = u_dt[:, 0, :], u_dt[:, 1, :]
                for tb in range(TB):
                    dve.scalar_tensor_tensor(
                        out=u[:, tb * DTW:(tb + 1) * DTW], in0=S[:, 2, T + tb * DTW:T + (tb + 1) * DTW],
                        scalar=rstd[:, tb:tb + 1], in1=dt_bias[:, :, :].rearrange("p a b -> p (a b)"),
                        op0=ALU.mult, op1=ALU.add).then_inc(dt_v, 1)
                dve.wait_ge(dt_v, 2)
                dve.tensor_scalar(m, u, -1.0, None, ALU.mult).then_inc(dt_v, 1)
                dve.wait_ge(dt_v, 3)
                dve.tensor_tensor(m, u, m, ALU.min).then_inc(dt_v, 1)
            if p == 6:
                u, m, e, t, sq, poly = (u_dt[:, n, :] for n in range(6))
                dve.wait_ge(dt_e, 3)
                dve.tensor_scalar(t, e, 2.0, None, ALU.add).then_inc(dt_v, 1)
                dve.wait_ge(dt_v, 5)
                dve.reciprocal(t, t).then_inc(dt_v, 1)
                dve.wait_ge(dt_v, 6)
                dve.tensor_tensor(t, t, e, ALU.mult).then_inc(dt_v, 1)
                dve.wait_ge(dt_v, 7)
                dve.tensor_tensor(sq, t, t, ALU.mult).then_inc(dt_v, 1)
                dve.wait_ge(dt_v, 8)
                dve.tensor_scalar(poly, sq, 1.0 / 15, None, ALU.mult).then_inc(dt_v, 1)
                for n, k in enumerate((13, 11, 9, 7, 5, 3)):
                    dve.wait_ge(dt_v, 9 + n)
                    dve.scalar_tensor_tensor(out=poly, in0=poly, scalar=1.0 / k, in1=sq,
                                             op0=ALU.add, op1=ALU.mult).then_inc(dt_v, 1)
                dve.wait_ge(dt_v, 15)
                dve.scalar_tensor_tensor(out=poly, in0=poly, scalar=1.0, in1=t,
                                         op0=ALU.add, op1=ALU.mult).then_inc(dt_v, 1)
                dve.tensor_scalar(m, u, 0.0, None, ALU.max).then_inc(dt_v, 1)
                dve.wait_ge(dt_v, 17)
                dve.scalar_tensor_tensor(out=dtv[:, :, :, :].rearrange("p b d h -> p (b d h)"), in0=poly,
                                         scalar=2.0, in1=m, op0=ALU.mult, op1=ALU.add).then_inc(dt_v, 1)
                dve.wait_ge(dt_v, 18)
                for tb in range(TB):
                    dve.scalar_tensor_tensor(out=av[:, tb, :, :], in0=dtv[:, tb, :, :], scalar=-1.0,
                                             in1=exp_a[:, :, :], op0=ALU.mult, op1=ALU.mult).then_inc(dt_v, 1)
                dve.wait_ge(dt_v, 20)
                dve.tensor_copy(av_hi[:, :, :, :], av[:, :, :, :]).then_inc(dt_v, 1)
                dve.wait_ge(dt_v, 21)
                dve.tensor_tensor(av_lo[:, :, :, :], av[:, :, :, :], av_hi[:, :, :, :].bitcast(F32), ALU.subtract
                                  ).then_inc(dt_v, 1)

        def decays(p, _, pr, pp):
            if p == 1:
                dve.wait_ge(dt_dec, 1)
                for c in range(TB):
                    dve.tensor_tensor(wdt[:, c, :], dtv[:, c, c, :], dec[:, c, :], ALU.mult).then_inc(dt_v, 1)

        def taps(g, pair):
            base = 2 * TAPS * pair
            for t in range(TAPS):
                for cc in range(2):
                    c = 2 * pair + cc
                    w = cw[:, ds(g, 1), c, t:t + 1].rearrange("p a b -> p (a b)")
                    bias = cw[:, ds(g, 1), c, TAPS:TAPS + 1].rearrange("p a b -> p (a b)")
                    if t == 0:
                        dve.tensor_scalar(acc[:, c, :], cv[:, c, 0:T], w, bias, ALU.mult, ALU.add
                                          ).then_inc(conv_v, 1)
                    else:
                        dve.wait_ge(conv_v, g * CONV_V + (base + 2 * t + cc - 1))
                        dve.scalar_tensor_tensor(out=acc[:, c, :], in0=cv[:, c, t:t + T], scalar=w,
                                                 in1=acc[:, c, :], op0=ALU.mult, op1=ALU.add
                                                 ).then_inc(conv_v, 1)

        def conv(p, g, pr, pp):
            if p == 2:
                if first(g):
                    dve.wait_ge(set_cv, 2)
                    dve.wait_ge(set_up, 5)
                dve.wait_ge(cv_made, 2 * g + 1)
                taps(g, 0)
            if p == 4:
                dve.wait_ge(cv_made, 2 * g + 2)
                taps(g, 1)
            if p == 6:
                dve.wait_ge(th_made, g + 1)
                if not first(g):
                    dve.wait_ge(off_mm, g)
                dve.scalar_tensor_tensor(out=cs[:, :, :].rearrange("p c t -> p (c t)"), in0=xt[:, :],
                                         scalar=1.0, in1=acc[:, :, :].rearrange("p c t -> p (c t)"),
                                         op0=ALU.add, op1=ALU.mult).then_inc(conv_v, 1)

        def scan(p, g, pr, pp):
            def step(n):
                return g * SCAN_V + n

            def heads(t, n):
                return t.unsqueeze(2).to_broadcast([P, 4, n])

            w = mw[:, 1 - pp, :, :, :]
            if p == 0:
                dve.wait_ge(score_mm, g + 1)
                for c in range(TB):
                    dve.wait_ge(mw_made, 2 * g + (c + 1))
                    dve.tensor_tensor(w[:, c, :, :], w[:, c, :, :],
                                      S[:, 0, c * P:(c + 1) * P].unsqueeze(1).to_broadcast([P, 4, P]), ALU.mult
                                      ).then_inc(scan_v, 1)
            if p == 1:
                dve.wait_ge(tm_made, 2 * g + 2)
                dve.wait_ge(dt_v, DT_A + 2)
                if not first(g):
                    dve.wait_ge(st_mm, g)
                for c in range(TB):
                    xs = tm[:, c, 0:4 * HD].rearrange("p (h d) -> p h d", h=4)
                    dve.tensor_tensor(xd[:, c, :, :], xs, heads(wdt[:, c, ds(g * 4, 4)], HD), ALU.mult
                                      ).then_inc(scan_v, 1)
            if p == 3:
                dve.wait_ge(scan_v, step(2))
                for c in range(TB):
                    dve.wait_ge(ex_made, 2 * g + (c + 1))
                    dve.tensor_tensor(w[:, c, :, :], w[:, c, :, :], ex[:, c, :, :], ALU.mult
                                      ).then_inc(scan_v, 1)
            if p == 6:
                dve.wait_ge(off_mm, g + 1)
                for_state = dec[:, 2:4, ds(g * 4, 4)].unsqueeze(3).to_broadcast([P, TB, 4, HD])
                dve.tensor_tensor(t1[:, :, :, :], S[:, 0, :].rearrange("p (c h d) -> p c h d", c=TB, h=4),
                                  for_state, ALU.mult).then_inc(scan_v, 1)
                dve.wait_ge(scan_v, step(7))
                dve.wait_ge(t2_made, 2 * g + 2)
                dve.tensor_tensor(t1[:, :, :, :], t1[:, :, :, :], t2[:, :, :, :], ALU.add).then_inc(scan_v, 1)
                dve.wait_ge(scan_v, step(8))
                dve.tensor_tensor(y_sb[:, :, ds(g * (4 * HD), 4 * HD)],
                                  S[:, 2, :].rearrange("p (c n) -> p c n", c=TB),
                                  t1[:, :, :, :].rearrange("p c h d -> p c (h d)"), ALU.add
                                  ).then_inc(scan_v, 1)

        def zgate(p, j, pr, pp):
            def step(n):
                return j * Z_V + n

            if p == 1:
                dve.wait_ge(taken[pp], pr + 1)
                dve.scalar_tensor_tensor(out=tmp_b[:, :, :], in0=tmp_b[:, :, :], scalar=1.0,
                                         in1=tmp_a[:, :, :], op0=ALU.add, op1=ALU.mult).then_inc(z_v, 1)
                dve.wait_ge(z_v, step(1))
                dve.wait_ge(scan_v, SCAN_V * (2 * j + 2))
                dve.tensor_tensor(tmp_a[:, :, :], tmp_b[:, :, :], y_sb[:, :, j * N:(j + 1) * N], ALU.mult
                                  ).then_inc(z_v, 1)
            if p == 3:
                dve.wait_ge(z_sq, 4 * (j + 1))
                dve.tensor_scalar(z_rs[:, :], z_ss[:, :], 1.0 / (4 * HD), EPS, ALU.mult, ALU.add
                                  ).then_inc(z_v, 1)
            if p == 4:
                dve.wait_ge(z_root, j + 1)
                for tb in range(TB):
                    for gg in range(2):
                        part = tmp_a[:, tb, gg * T:(gg + 1) * T]
                        dve.tensor_scalar(part, part, z_rs[:, 2 * tb + gg:2 * tb + gg + 1], 0.5,
                                          ALU.mult, ALU.mult).then_inc(z_v, 1)
            if p == 7:
                split_low(TS_Z + j, b_hi, b_lo, 4 * j, gain=2)

        def rope(p, n, pr, pp):
            qk = 0 if n else 1

            def step(k):
                return n * ROPE_V + k

            if p == 1:
                for tb in range(TB):
                    dve.wait_ge(r_sq, 2 * n + tb + 1)
                    dve.tensor_reduce(q_ss[:, tb, :], tmp_b[:, tb, :].rearrange("p (h d) -> p h d", h=4),
                                      AX_X, ALU.add).then_inc(r_v, 1)
                dve.wait_ge(r_v, step(2))
                dve.tensor_scalar(q_rs[:, :, :], q_ss[:, :, :], 1.0 / AD, EPS, ALU.mult, ALU.add
                                  ).then_inc(r_v, 1)
            if p in (3, 4):
                tb = p - 3
                dve.wait_ge(taken[pp], pr + 1)
                own = tmp_a[:, tb, :].rearrange("p (h d) -> p h d", h=4)
                cross = tmp_b[:, tb, :].rearrange("p (h d) -> p h d", h=4)
                base = 3 + 4 * tb
                for e in range(2):
                    dve.tensor_tensor(cross[:, :, e:AD:2], own[:, :, 1 - e:AD:2],
                                      rope_t[:, qk, 1, tb, e:AD:2].unsqueeze(1).to_broadcast([P, 4, AD // 2]),
                                      ALU.mult).then_inc(r_v, 1)
                dve.wait_ge(r_v, step(base + 2))
                dve.tensor_tensor(own, own, rope_t[:, qk, 0, tb, :].unsqueeze(1).to_broadcast([P, 4, AD]),
                                  ALU.mult).then_inc(r_v, 1)
                dve.wait_ge(r_v, step(base + 3))
                dve.tensor_tensor(own, own, cross, ALU.add).then_inc(r_v, 1)

        def attend(p, g, pr, pp):
            def biggest(h):
                dve.wait_ge(at_sc, 4 * g + h + 1)
                dve.tensor_reduce(mx[:, h, :], S[:, h % 2, :].rearrange("p (b s) -> p b s", b=TB),
                                  AX_X, ALU.max).then_inc(at_max, 1)
                dve.wait_ge(at_max, 8 * g + 2 * h + 1)
                dve.tensor_scalar(nb[:, h, :], mx[:, h, :], -SCALE, None, ALU.mult).then_inc(at_max, 1)

            def normalise(h):
                dve.wait_ge(at_exp, 8 * g + 2 * h + 2)
                dve.reciprocal(rden[:, h, :], den[:, h, :]).then_inc(at_v, 1)
                dve.wait_ge(at_v, (4 * g + h) * AT_V + 1)
                for tb in range(TB):
                    dve.tensor_scalar(prob[:, h, tb, :], prob[:, h, tb, :], rden[:, h, tb:tb + 1], None,
                                      ALU.mult).then_inc(at_v, 1)

            def low(pair):
                dve.wait_ge(at_hi, 2 * g + pair + 1)
                k = 4 * g + 2 * pair
                dve.tensor_tensor(c_lo[:, k:k + 2, :], S[:, 3, :].rearrange("p (c t) -> p c t", c=2),
                                  c_hi[:, k:k + 2, :].bitcast(F32), ALU.subtract).then_inc(at_lo, 1)

            if p == 0:
                biggest(0)
                biggest(1)
            if p == 1:
                normalise(0)
                biggest(2)
                normalise(1)
                biggest(3)
            if p == 2:
                normalise(2)
                normalise(3)
            if p == 5:
                low(0)
            if p == 7:
                low(1)

        def gated(dst, pr, pp):
            dve.wait_ge(used, done(pr, pp))
            dve.wait_ge(taken[pp], pr)
            for tb in range(TB):
                last = dve.scalar_tensor_tensor(out=dst[:, tb, :], in0=dst[:, tb, :], scalar=1.0,
                                                in1=product(pp, tb), op0=ALU.add, op1=ALU.mult)
            last.then_inc(taken[pp], 1)

        def gated_a(p, j, pr, pp):
            if p == 0:
                gated(tmp_a, pr, pp)

        def merged(p, j, pr, pp):
            if p == 0:
                gated(tmp_b, pr, pp)
                dve.wait_ge(taken[pp], pr + 1)
                dve.tensor_tensor(tmp_b[:, :, :], tmp_b[:, :, :], tmp_a[:, :, :], ALU.add).then_inc(merge_v, 1)
            if p == 2:
                split_low(j + TS_MERGED, m_hi, m_lo, j * 4, factor=0.5)

        def add_product(j, pr, pp):
            dve.wait_ge(used, done(pr, pp))
            for tb in range(TB):
                part = x_sb[:, tb, j * N:(j + 1) * N]
                last = dve.tensor_tensor(part, part, product(pp, tb), ALU.add)
            last.then_inc(taken[pp], 1)

        def residual(p, j, pr, pp):
            if p == 0:
                add_product(j, pr, pp)
            if p == 2:
                split_low(TS_X2 + j, b_hi, b_lo, 4 * j, gain=1)
            if p == 4 and j == 3:
                dve.wait_ge(sq_x, 5 * TB)
                dve.tensor_reduce(x_ss[:, :], rows_ss[:, :, :], AX_X, ALU.add).then_inc(var_x, 1)
                dve.wait_ge(var_x, 3)
                dve.tensor_scalar(x_var[:, :], x_ss[:, :], 1.0 / D, EPS, ALU.mult, ALU.add).then_inc(var_x, 1)

        def hidden(p, idx, pr, pp):
            g, j = idx
            if p == 2:
                split_low(g * 4 + (TS_HID + j), a_hi, a_lo, 4 * j)

        def add(p, j, pr, pp):
            if p == 0:
                add_product(j, pr, pp)

        table = {f.__name__: f for f in (rates, decays, conv, scan, zgate, rope, attend, gated_a, merged, residual,
                                         hidden, add)}

        def window(r, par, kind, idx, sides):
            for p in range(PIECES):
                q = p + LEAD
                if not (isinstance(r, int) and 2 * r + par == U_END - 1 and q >= PIECES):
                    split(piece_number(r, par, q), q % RING, 2 * N)
                for name, at in sides:
                    if name in table:
                        table[name](p, at, *previous(r, par))

        walk(dve, window)
        add_product(3, U_END // 2 - 1, 1)
        dve.wait_ge(sq_x, 6 * TB)
        dve.tensor_scalar(x_var[:, :], x_ss[:, :], 1.0 / D, EPS, ALU.mult, ALU.add).then_inc(var_x, 1)
        dve.wait_ge(rstd_x, 3)
        dve.wait_ge(s_g_last, 16)
        for tb in range(TB):
            dve.scalar_tensor_tensor(out=fin[:, tb, :], in0=x_sb[:, tb, :], scalar=rstd_out[:, tb:tb + 1],
                                     in1=g_last[:, :], op0=ALU.mult, op1=ALU.mult).then_inc(fin_v, 1)

    @block.gpsimd
    def _(pool):
        pool.memset(minus_half[:, :], -0.5).then_inc(expo, 1)
        pool.wait_ge(expo, 1)

        def inverse_root(dst, src, n):
            return pool.tensor_tensor(dst, src, minus_half[:, 0:n], ALU.pow)

        def rates(p, _, pr, pp):
            if p == 2:
                pool.wait_ge(var_x, 1)
                inverse_root(rstd[:, :], x_var[:, :], TB).then_inc(rstd_x, 1)

        def masked_rates(g, c):
            for d in range(2):
                for part, rate in ((mv_hi, av_hi), (mv_lo, av_lo)):
                    pool.tensor_tensor(
                        part[:, c, d, :, :], masks[:, 2 + d, :].unsqueeze(1).to_broadcast([P, 4, P]),
                        rate[:, c, d, ds(g * 4, 4)].bitcast(F32).unsqueeze(2).to_broadcast([P, 4, P]), ALU.mult
                    ).then_inc(mv_made, 1)

        def masked_dt(g, parity, c):
            for d, dst in enumerate((mw[:, parity, c, :, :], mw_b)):
                pool.tensor_tensor(dst, masks[:, 2 + d, :].unsqueeze(1).to_broadcast([P, 4, P]),
                                   dtv[:, c, d, ds(g * 4, 4)].unsqueeze(2).to_broadcast([P, 4, P]), ALU.mult
                                   ).then_inc(mw_steps, 1)
            pool.wait_ge(mw_steps, 4 * g + (2 * c + 2))
            pool.tensor_tensor(mw[:, parity, c, :, :], mw[:, parity, c, :, :], mw_b, ALU.add
                               ).then_inc(mw_made, 1)

        def decays(p, _, pr, pp):
            if p == 0:
                pool.wait_ge(s_masks, 16)
                pool.wait_ge(dt_v, DT_A)
                for c in range(TB):
                    masked_rates(0, c)
                masked_dt(0, 0, 0)
                pool.wait_ge(mw_made, 1)
                masked_dt(0, 0, 1)

        def scan(p, g, pr, pp):
            if p == 0:
                pool.wait_ge(tm_made, 2 * g + 2)
                if not first(g):
                    pool.wait_ge(scan_v, g * SCAN_V)
                for c in range(TB):
                    pool.tensor_tensor(t2[:, c, :, :], tm[:, c, 0:4 * HD].rearrange("p (h d) -> p h d", h=4),
                                       dskip[:, ds(g * 4, 4)].unsqueeze(2).to_broadcast([P, 4, HD]), ALU.mult
                                       ).then_inc(t2_made, 1)
                if not (isinstance(g, int) and g == GROUPS - 1):
                    for c in range(TB):
                        pool.wait_ge(seg_mm, 2 * g + (c + 1))
                        masked_rates(g + 1, c)
                    if not first(g):
                        pool.wait_ge(y_mm, 2 * g)
                    for c in range(TB):
                        pool.wait_ge(mw_made, 2 * g + (c + 2))
                        masked_dt(g + 1, pp, c)

        def zgate(p, j, pr, pp):
            if p == 3:
                pool.wait_ge(z_v, j * Z_V + 3)
                inverse_root(z_rs[:, :], z_rs[:, :], 4).then_inc(z_root, 1)

        def rope(p, n, pr, pp):
            if p == 1:
                flat = q_rs[:, :, :].rearrange("p b h -> p (b h)")
                pool.wait_ge(r_v, n * ROPE_V + 3)
                inverse_root(flat, flat, 2 * 4).then_inc(r_root, 1)
                pool.wait_ge(r_root, 2 * n + 1)
                pool.tensor_tensor(q_rs[:, :, :], q_rs[:, :, :],
                                   rstd[:, :].unsqueeze(2).to_broadcast([P, TB, 4]), ALU.mult
                                   ).then_inc(r_root, 1)

        def attend(p, g, pr, pp):
            if p == 0:
                pool.wait_ge(taken[1], U_V // 2 + 1)
                if g:
                    pool.wait_ge(at_pv, 4 * g)
                pool.tensor_copy(vg[:, :, :], v_sb[:, :, g, :]).then_inc(vg_made, 1)

        def residual(p, j, pr, pp):
            if p == 4 and j == 3:
                pool.wait_ge(var_x, 4)
                inverse_root(rstd_mlp[:, :], x_var[:, :], TB).then_inc(rstd_x, 1)

        table = {f.__name__: f for f in (rates, decays, scan, zgate, rope, attend, residual)}

        def window(r, par, kind, idx, sides):
            for p in range(PIECES):
                for name, at in sides:
                    if name in table:
                        table[name](p, at, *previous(r, par))

        walk(pool, window)
        pool.wait_ge(var_x, 5)
        inverse_root(rstd_out[:, :], x_var[:, :], TB).then_inc(rstd_x, 1)

    @block.tensor
    def _(pe):
        operand = {"ssm_up": (b_hi, b_lo), "attn_up": (c_hi, c_lo), "out": (m_hi, m_lo),
                   "mlp_in": (b_hi, b_lo), "mlp_out": (a_hi, a_lo)}

        def three_passes(out_ap, k, tb, hi, lo, w_hi, w_lo, start, stop):
            cols = slice(tb * P, (tb + 1) * P)
            pe.matmul(out_ap, hi[:, k, cols], w_hi, start=start, stop=False)
            pe.matmul(out_ap, hi[:, k, cols], w_lo, start=False, stop=False)
            return pe.matmul(out_ap, lo[:, k, cols], w_hi, start=False, stop=stop)

        def transpose_round(src):
            for c in range(4):
                for tb in range(TB):
                    last = pe.transpose(S[:, c // 2, c % 2 * T + tb * P:c % 2 * T + (tb + 1) * P],
                                        src(c, tb), ident[:, :])
            return last

        def split_round(rnd, src):
            pe.wait_ge(ts_lo, rnd)
            transpose_round(src).then_inc(ts_t, 1)

        pe.wait_ge(s_ident, 16)
        pe.wait_ge(s_gains, 16 * 3)
        pe.transpose(S[:, 3, 0:3 * KT], param_rows[0:3 * KT, 0, :], ident[0:3 * KT, 0:3 * KT]).then_inc(rows_t, 1)
        for j in range(4):
            pe.wait_ge(s_x[j], 16)
            if j == 3:
                pe.wait_ge(ts_lo, TS_X + 1)
            for c in range(4):
                for tb in range(TB):
                    last = pe.transpose(x_bank(j, c, slice(tb * P, (tb + 1) * P)),
                                        x_sb[:, tb, (4 * j + c) * P:(4 * j + c + 1) * P], ident[:, :])
            last.then_inc(ts_t, 1)
        pe.wait_ge(s_taps, 16 * 3)
        for n in (1, 2):
            at = 3 * KT + (n - 1) * 6 * KT
            last = pe.transpose(S[:, 3, at:at + 6 * KT], param_rows[0:6 * KT, n, :], ident[0:6 * KT, 0:6 * KT])
        last.then_inc(rows_t, 1)
        pe.wait_ge(lo_made, 1)
        for k in range(KT):
            if k % 4 == 0:
                pe.wait_ge(ts_lo, TS_X + k // 4 + 1)
            cols = slice(k * DTW, (k + 1) * DTW)
            into = S[0:DTW, 2, 0:T]
            pe.matmul(into, whi[:, RING - 1, cols], a_hi[:, k, :], start=(k == 0), stop=False)
            pe.matmul(into, whi[:, RING - 1, cols], a_lo[:, k, :], start=False, stop=False)
            last = pe.matmul(into, wlo[:, RING - 1, cols], a_hi[:, k, :], start=False, stop=(k == KT - 1))
        last.then_inc(used, 1)

        def rates(p, _, pr, pp):
            if p == 1:
                pe.wait_ge(dt_e, 1)
                for tb in range(TB):
                    last = pe.transpose(S[:, 2, T + tb * DTW:T + (tb + 1) * DTW],
                                        dt_rows[:, tb * P:(tb + 1) * P], ident[0:DTW, 0:DTW])
                last.then_inc(dt_t, 1)

        def decays(p, _, pr, pp):
            if p == 0:
                pe.wait_ge(dt_v, DT_A)
                pe.wait_ge(s_masks, 16)
                pe.wait_ge(set_up, 5)
                for n, (m, c, d) in enumerate(((0, 0, 0), (1, 1, 1), (3, 0, 1), (2, 1, 0))):
                    last = pe.matmul(S[:, 3, n * HEADS:(n + 1) * HEADS], masks[:, m, :], av[:, c, d, :],
                                     start=True, stop=True)
                last.then_inc(dt_mm, 1)

        def conv(p, g, pr, pp):
            if p == 1:
                pe.wait_ge(taken[pp], pr + 1)
                if not first(g):
                    pe.wait_ge(scan_v, g * SCAN_V - SCAN_V + 2)
                    pe.wait_ge(tm_made, 2 * g)
                transpose_round(lambda c, tb: xt[:, tb * N + c * P:tb * N + (c + 1) * P]).then_inc(conv_t, 1)
            if p == 7:
                pe.wait_ge(conv_v, g * CONV_V + CONV_V)
                if first(g):
                    pe.wait_ge(dt_dec, 1)
                else:
                    pe.wait_ge(st_made, g)
                for tb in range(TB):
                    for c in range(3):
                        last = pe.transpose(S[:, 1 + 2 * tb, c * P:(c + 1) * P],
                                            cs[:, c, tb * P:(tb + 1) * P], ident[:, :])
                last.then_inc(back_t, 1)

        def scan(p, g, pr, pp):
            if p == 0:
                if not first(g):
                    pe.wait_ge(scan_v, g * SCAN_V)
                for c in range(TB):
                    last = pe.matmul(S[:, 0, c * P:(c + 1) * P], cs[:, 2, c * P:(c + 1) * P],
                                     cs[:, 3, c * P:(c + 1) * P], start=True, stop=True)
                last.then_inc(score_mm, 1)
            if p in (1, 2):
                c = p - 1
                pe.wait_ge(mv_made, 8 * g + (4 * c + 4))
                if c == 1:
                    pe.wait_ge(tm_made, 2 * g + 2)
                else:
                    pe.wait_ge(dt_v, 2)
                if first(g):
                    pe.wait_ge(masks_made, 1)
                for n in range(4):
                    d, part = n // 2, (mv_hi, mv_lo)[n % 2]
                    last = pe.matmul(S[:, 2 + c, :], masks_r[:, d, :],
                                     part[:, c, d, :, :].rearrange("p h l -> p (h l)"),
                                     start=(n == 0), stop=(n == 3))
                last.then_inc(seg_mm, 1)
            if p == 3:
                pe.wait_ge(scan_v, g * SCAN_V + 4)
                pe.wait_ge(ex_made, 2 * g + 2)
                for c in range(TB):
                    last = pe.matmul(S[:, 3, c * 4 * HD:(c + 1) * 4 * HD], tm[:, c, 2 * P:3 * P],
                                     xd[:, c, :, :].rearrange("p h d -> p (h d)"), start=True, stop=True)
                last.then_inc(st_mm, 1)
            if p in (4, 5):
                c = p - 4
                pe.wait_ge(scan_v, g * SCAN_V + (4 + (c + 1)))
                for h in range(4):
                    last = pe.matmul(S[:, 2, (4 * c + h) * HD:(4 * c + h + 1) * HD],
                                     mw[:, 1 - pp, c, h, :], tm[:, c, h * HD:(h + 1) * HD],
                                     start=True, stop=True)
                last.then_inc(y_mm, 1)
            if p == 5:
                pe.wait_ge(st_made, g + 1)
                if not (isinstance(g, int) and g == GROUPS - 1):
                    pe.wait_ge(cv_made, 2 * g + 3)
                for c in range(TB):
                    last = pe.matmul(S[:, 0, c * 4 * HD:(c + 1) * 4 * HD], cs[:, 3, c * P:(c + 1) * P],
                                     st[:, 1 - c, :], start=True, stop=True)
                last.then_inc(off_mm, 1)

        def zgate(p, j, pr, pp):
            if p == 6:
                pe.wait_ge(z_v, (j + 1) * Z_V)
                if j == 0:
                    pe.wait_ge(scan_v, SCAN_V * GROUPS)
                split_round(TS_Z + j, lambda c, tb: tmp_a[:, tb, c * P:(c + 1) * P])

        def rope(p, n, pr, pp):
            if p == 6:
                pe.wait_ge(r_v, (n + 1) * ROPE_V)
                if n == 0:
                    pe.wait_ge(ts_lo, TS_MERGED)
                else:
                    pe.wait_ge(r_made, 2 * n)
                if n >= 2:
                    pe.wait_ge(at_exp, 8 * (n - 1))
                transpose_round(lambda c, tb: tmp_a[:, tb, c * P:(c + 1) * P]).then_inc(r_t, 1)

        def attend(p, g, pr, pp):
            def scores(h):
                pe.wait_ge(r_made, 2 * (g + 2))
                if h >= 2:
                    pe.wait_ge(at_exp, 8 * g + 2 * (h - 1))
                for tb in range(TB):
                    last = pe.matmul(S[:, h % 2, tb * T:(tb + 1) * T], qT[:, h, tb * P:(tb + 1) * P],
                                     kT[:, g, :], start=True, stop=True)
                last.then_inc(at_sc, 1)

            def turn(h):
                pe.wait_ge(at_v, (4 * g + h + 1) * AT_V)
                if 4 * g + h:
                    pe.wait_ge(at_pt, 4 * g + h)
                for sb in range(TB):
                    for tb in range(TB):
                        last = pe.transpose(S[:, 2, sb * T + tb * P:sb * T + (tb + 1) * P],
                                            prob[:, h, tb, sb * P:(sb + 1) * P], ident[:, :])
                last.then_inc(at_t, 1)

            def weigh(h):
                pe.wait_ge(at_pt, 4 * g + h + 1)
                pe.wait_ge(vg_made, g + 1)
                if 2 * g + h // 2:
                    pe.wait_ge(at_lo, 2 * g + h // 2)
                for sb in range(TB):
                    last = pe.matmul(S[:, 3, h % 2 * T:(h % 2 + 1) * T], vg[:, sb, :], pT[:, h % 2, sb, :],
                                     start=(sb == 0), stop=(sb == TB - 1))
                last.then_inc(at_pv, 1)

            if p in (0, 1):
                scores(2 * p)
                scores(2 * p + 1)
            if p == 2:
                turn(0)
            if p == 3:
                turn(1)
                weigh(0)
            if p == 4:
                weigh(1)
                turn(2)
            if p == 5:
                turn(3)
            if p == 6:
                weigh(2)
                weigh(3)

        def merged(p, j, pr, pp):
            if p == 1:
                pe.wait_ge(merge_v, j + 1)
                pe.wait_ge(at_exp, 8 * KVH)
                split_round(j + TS_MERGED, lambda c, tb: tmp_b[:, tb, c * P:(c + 1) * P])

        def residual(p, j, pr, pp):
            if p == 1:
                pe.wait_ge(taken[pp], pr + 1)
                split_round(TS_X2 + j, lambda c, tb: x_sb[:, tb, (4 * j + c) * P:(4 * j + c + 1) * P])

        def hidden(p, idx, pr, pp):
            g, j = idx
            if p == 1:
                pe.wait_ge(hid_sq, g * 4 + (j + 1))
                split_round(g * 4 + (TS_HID + j), lambda c, tb: tmp_b[:, tb, c * P:(c + 1) * P])

        table = {f.__name__: f for f in (rates, decays, conv, scan, zgate, rope, attend, merged, residual, hidden)}

        def window(r, par, kind, idx, sides):
            hi, lo = operand.get(kind, (a_hi, a_lo))
            if not (isinstance(r, int) and r == 0):
                pe.wait_ge(taken[par], r)
            rounds = {"ssm_up": TS_MERGED, "out": TS_X2, "mlp_in": TS_HID}.get(kind)
            if kind == "mlp_out":
                rounds = idx[0] * 4 + (TS_HID + 4)
            late = (kind == "out" and idx == 0) or (kind == "mlp_in" and first(idx[0]) and idx[1] == 0) or (
                kind == "mlp_out" and idx[1] == 0)
            for p in range(PIECES):
                if p == 0 and rounds is not None:
                    pe.wait_ge(ts_lo, rounds - 1 if late else rounds)
                if p == PIECES - 2 and late:
                    pe.wait_ge(ts_lo, rounds)
                if p == 0 and kind == "attn_up":
                    pe.wait_ge(at_lo, 2 * KVH)
                pe.wait_ge(lo_made, piece_number(r, par, p) + 1)
                for kk in range(2):
                    k = 2 * p + kk
                    cols = slice(kk * N, (kk + 1) * N)
                    for tb in range(TB):
                        last = three_passes(product(par, tb), k, tb, hi, lo, whi[:, p % RING, cols],
                                            wlo[:, p % RING, cols], k == 0, k == KT - 1)
                last.then_inc(used, 1)
                for name, at in sides:
                    if name in table:
                        table[name](p, at, *previous(r, par))

        walk(pe, window)

    keep.close()


def shape_constants():
    grid_w, theta, half = 64, 10000.0, AD // 2
    i = np.arange(P)
    t, s = i[:, None], i[None, :]
    parts = [t == s, t > s, t < s, t <= s, t >= s]
    inv = (1.0 / (theta ** (np.arange(0, half, 2, dtype=np.float32) / np.float32(half)))).astype(np.float32)
    tok = np.arange(T)
    row, col = (tok // grid_w).astype(np.float32), (tok % grid_w).astype(np.float32)
    ang = np.concatenate([row[:, None] * inv, col[:, None] * inv], axis=1)
    cos = np.repeat(np.cos(ang), 2, axis=1)
    sin = np.stack([-np.sin(ang), np.sin(ang)], axis=-1).reshape(T, AD)
    for table in (cos, sin):
        parts += [table[:P], table[P:]]
    return np.concatenate([np.asarray(a, np.float32) for a in parts], axis=1)


_INS = ["x", "g_mix", "w_in", "conv_w", "conv_b", "dt_bias_f", "dt_bias_b", "a_log_f", "a_log_b", "d_skip",
        "ssm_norm_g", "q_norm_g", "k_norm_g", "w_ssm_up", "w_attn_up", "w_out", "g_mlp", "w_mlp_in",
        "w_mlp_out", "g_final"]


def kernel(**inputs):
    import concourse.bacc as bacc
    from concourse.bass_utils import run_bass_kernel_spmd

    nc = bacc.Bacc("TRN2", target_bir_lowering=False, num_devices=1)
    arrays, args = {}, []
    for name in _INS + ["consts"]:
        a = np.ascontiguousarray(shape_constants() if name == "consts" else inputs[name])
        arrays[f"in_{name}"] = a
        args.append(nc.dram_tensor(f"in_{name}", a.shape, mybir.dt.from_np(a.dtype), kind="ExternalInput").ap())
    out = nc.dram_tensor("out_0", (1, T, D), F32, kind="ExternalOutput").ap()
    build(nc, *args, out)
    r = run_bass_kernel_spmd(nc, [arrays], core_ids=[0])
    return r.results[0]["out_0"]
```

```python
from contextlib import ExitStack

import concourse.bass as bass
import numpy as np
from concourse import mybir

ALU = mybir.AluOpType
ACT = mybir.ActivationFunctionType
AX_X = mybir.AxisListType.X
F32 = mybir.dt.float32
F32R = mybir.dt.float32r
ds = bass.ds

P = 128
D = 2048
T = 256
TB = T // P
KT = D // P
N = 512
PIECES = 8
RING = 4
LEAD_HI = 3
LEAD_LO = 2
HEADS = 32
HD = 64
GROUPS = 8
TAPS = 5
QH, KVH, AD = 16, 4, 128
D_FF = 4 * D
EPS = 1e-6
SCALE = float(AD) ** -0.5
COL_Z = 0
COL_XS = COL_Z + D
COL_B = COL_XS + D
COL_C = COL_B + GROUPS * P
COL_DT = COL_C + GROUPS * P
COL_Q = COL_DT + 2 * HEADS
COL_K = COL_Q + QH * AD
COL_V = COL_K + KVH * AD
COL_GA = COL_V + KVH * AD
COL_GB = COL_GA + D
DTW = 2 * HEADS

U_XBC, U_Z, U_K, U_V, U_Q, U_GATE, U_OUT, U_MLP = 0, 8, 12, 13, 14, 18, 34, 38
U_END = U_MLP + 32
TS_X, TS_Z, TS_MERGED, TS_X2, TS_HID = 0, 4, 8, 12, 16
THREES = 9


def walk(eng, window):
    window(0, 0, "xbc", 0, [("rates", 0)])
    window(0, 1, "xbc", 1, [("conv", 0), ("decays", 0)])
    window(1, 0, "xbc", 2, [("conv", 1), ("scan", 0)])
    window(1, 1, "xbc", 3, [("conv", 2), ("scan", 1)])
    with eng.Fori(1, 3) as i:
        window(i + 1, 0, "xbc", 2 * i + 2, [("conv", 2 * i + 1), ("scan", 2 * i)])
        window(i + 1, 1, "xbc", 2 * i + 3, [("conv", 2 * i + 2), ("scan", 2 * i + 1)])
    window(4, 0, "z", 0, [("conv", 7), ("scan", 6)])
    window(4, 1, "z", 1, [("zgate", 0), ("scan", 7)])
    window(5, 0, "z", 2, [("zgate", 1)])
    window(5, 1, "z", 3, [("zgate", 2)])
    window(6, 0, "k", 0, [("zgate", 3)])
    window(6, 1, "v", 0, [("rope", 0)])
    window(7, 0, "q", 0, [("values", 0)])
    window(7, 1, "q", 1, [("rope", 1)])
    window(8, 0, "q", 2, [("attend", 0), ("rope", 2)])
    window(8, 1, "q", 3, [("attend", 1), ("rope", 3)])
    window(9, 0, "ga", 0, [("attend", 2), ("rope", 4)])
    window(9, 1, "gb", 0, [("attend", 3), ("gate_a", 0)])
    with eng.Fori(0, 3) as j:
        window(2 * j + 10, 0, "ssm_up", j, [("gate_b", j)])
        window(2 * j + 10, 1, "attn_up", j, [("gated_a", j)])
        window(2 * j + 11, 0, "ga", j + 1, [("merged", j)])
        window(2 * j + 11, 1, "gb", j + 1, [("gate_a", j + 1)])
    window(16, 0, "ssm_up", 3, [("gate_b", 3)])
    window(16, 1, "attn_up", 3, [("gated_a", 3)])
    window(17, 0, "out", 0, [("merged", 3)])
    window(17, 1, "out", 1, [("residual", 0)])
    window(18, 0, "out", 2, [("residual", 1)])
    window(18, 1, "out", 3, [("residual", 2)])
    window(19, 0, "mlp_in", (0, 0), [("residual", 3)])

    def rest_of_hidden_group(g, add):
        for j in range(1, 4):
            window(4 * g + 19 + j // 2, j % 2, "mlp_in", (g, j), [("hidden", (g, j - 1))])
        window(4 * g + 21, 0, "mlp_out", (g, 0), [("hidden", (g, 3))])
        for j in range(1, 4):
            window(4 * g + 21 + j // 2, j % 2, "mlp_out", (g, j), [(add, j - 1)])

    with eng.Fori(0, 3) as g:
        rest_of_hidden_group(g, "add")
        window(4 * g + 23, 0, "mlp_in", (g + 1, 0), [("add", 3)])
    rest_of_hidden_group(3, "finish")


def piece_number(r, par, p):
    return r * (2 * PIECES) + (PIECES * par + p)


def landed_count(r, par, p, threes):
    uses = r * (2 * PIECES // RING) + (PIECES // RING * par + p // RING + 1)
    if threes:
        return uses * 48
    return uses * 16 + 32 * THREES * PIECES // RING


def previous(r, par):
    return (r, 0) if par else (r - 1, 1)


def first(idx):
    return isinstance(idx, int) and idx == 0


def build(nc, x, g_mix, w_in, conv_w, conv_b, dt_bias_f, dt_bias_b, a_log_f, a_log_b, d_skip,
          ssm_norm_g, q_norm_g, k_norm_g, w_ssm_up, w_attn_up, w_out, g_mlp, w_mlp_in, w_mlp_out,
          g_final, consts, out):
    top = [-(-nc.sbuf_base // 64) * 64]

    def place(name, shape, dt=F32):
        n = 4
        for s in shape[1:]:
            n *= s
        t = nc.alloc_sbuf_tensor_at(name, shape, dt, offset=top[0])
        top[0] += -(-n // 32) * 32
        return t

    raw = place("raw", [P, RING, 2 * N])
    whi = place("whi", [P, RING, 2 * N], F32R)
    wlo = place("wlo", [P, RING, 2 * N], F32R)
    a_hi = place("a_hi", [P, KT, T], F32R)
    a_lo = place("a_lo", [P, KT, T], F32R)
    x_sb = place("x_sb", [P, TB, D])
    tmp_a = place("tmp_a", [P, TB, N])
    tmp_b = place("tmp_b", [P, TB, N])
    ident = place("ident", [P, P])
    gains = place("gains", [P, 3 * KT])
    rope_t = place("rope_t", [P, 2, 2, TB, AD])
    rstd = place("rstd", [P, TB])
    half_rstd = place("half_rstd", [P, TB])
    rstd_mlp = place("rstd_mlp", [P, TB])
    rstd_out = place("rstd_out", [P, TB])
    x_ss = place("x_ss", [P, TB])
    x_var = place("x_var", [P, TB])
    rows_ss = place("rows_ss", [P, TB, 4])
    z_ss = place("z_ss", [P, 4])
    z_rs = place("z_rs", [P, 4])
    q_ss = place("q_ss", [P, TB, 4])
    q_rs = place("q_rs", [P, TB, 4])
    minus_half = place("minus_half", [P, 8])

    region_b = top[0]
    xt = place("xt", [P, TB * N])
    cv = place("cv", [P, 4, T + TAPS - 1])
    acc = place("acc", [P, 4, T])
    cw = place("cw", [P, GROUPS, 4, TAPS + 1])
    param_rows = place("param_rows", [3 * 2 * KT, 3, P])
    rope_raw = place("rope_raw", [P, 2, TB, AD])
    qk_gain = place("qk_gain", [P, 2, AD])
    end_b = top[0]
    top[0] = region_b
    b_hi = place("b_hi", [P, KT, T], F32R)
    b_lo = place("b_lo", [P, KT, T], F32R)
    assert end_b <= top[0]

    region_y = top[0]
    y_sb = place("y_sb", [P, TB, D])
    end_y = top[0]
    top[0] = region_y
    dt_raw = place("dt_raw", [P, KT, DTW])
    dt_hi = place("dt_hi", [P, KT, DTW], F32R)
    dt_lo = place("dt_lo", [P, KT, DTW], F32R)
    assert top[0] <= end_y
    top[0] = region_y
    kT_hi = place("kT_hi", [P, KVH, T], F32R)
    v_sb = place("v_sb", [P, TB, KVH, AD])
    prob = place("prob", [P, 4, TB, T])
    assert top[0] <= end_y
    top[0] = region_y
    m_hi = place("m_hi", [P, KT, T], F32R)
    assert top[0] <= end_y
    top[0] = end_y

    region_r = top[0]
    masks = place("masks", [P, 4, P])
    cs = place("cs", [P, 4, T])
    tm = place("tm", [P, TB, 3 * P])
    masks_r = place("masks_r", [P, 2, P], F32R)
    squares = nc.alloc_sbuf_tensor_at("squares", [P, TB, D], F32, offset=top[0])
    mv_hi = place("mv_hi", [P, TB, 2, 4, P], F32R)
    mv_lo = place("mv_lo", [P, TB, 2, 4, P], F32R)
    ex = place("ex", [P, TB, 4, P])
    mw = place("mw", [P, 2, TB, 4, P])
    mw_b = tmp_b[:, 0, :].rearrange("p (h l) -> p h l", h=4)
    xd = place("xd", [P, TB, 4, HD])
    st = place("st", [P, TB, 4 * HD])
    t1 = place("t1", [P, TB, 4, HD])
    t2 = place("t2", [P, TB, 4, HD])
    dt_bias = place("dt_bias", [P, 2, HEADS])
    exp_a = place("exp_a", [P, 2, HEADS])
    dskip = place("dskip", [P, HEADS])
    dtv = place("dtv", [P, TB, 2, HEADS])
    av = place("av", [P, TB, 2, HEADS])
    av_hi = place("av_hi", [P, TB, 2, HEADS], F32R)
    av_lo = place("av_lo", [P, TB, 2, HEADS], F32R)
    dec = place("dec", [P, 4, HEADS])
    wdt = place("wdt", [P, TB, HEADS])
    assert top[0] <= nc.sbuf_usable_end, (top[0], nc.sbuf_usable_end)
    top[0] = region_r
    c_hi = place("c_hi", [P, KT, T], F32R)
    c_lo = place("c_lo", [P, KT, T], F32R)
    region_r2 = top[0]
    qT_hi = place("qT_hi", [P, 4, T], F32R)
    qT_lo = place("qT_lo", [P, 4, T], F32R)
    kT_lo = place("kT_lo", [P, KVH, T], F32R)
    pT_hi = place("pT_hi", [P, TB, T], F32R)
    pT_lo = place("pT_lo", [P, TB, T], F32R)
    vg_hi = place("vg_hi", [P, TB, AD], F32R)
    vg_lo = place("vg_lo", [P, TB, AD], F32R)
    mx = place("mx", [P, 4, TB])
    nb = place("nb", [P, 4, TB])
    den = place("den", [P, 4, TB])
    rden = place("rden", [P, 4, TB])
    assert top[0] <= nc.sbuf_usable_end, (top[0], nc.sbuf_usable_end)
    top[0] = region_r2
    m_lo = place("m_lo", [P, KT, T], F32R)
    assert top[0] <= nc.sbuf_usable_end, (top[0], nc.sbuf_usable_end)
    top[0] = region_r
    g_last = place("g_last", [P, D])
    fin = place("fin", [P, TB, D])

    keep = ExitStack()

    def sem(name):
        return keep.enter_context(nc.semaphore(name))

    G = keep.enter_context(nc.psum_tensor("G", [P, 4, N], F32))
    S = keep.enter_context(nc.psum_tensor("S", [P, 4, N], F32))

    s_ident, s_g_mix, s_rows, s_masks, s_rope, s_dt_in = [
        sem(f"s_{n}") for n in ("ident", "g_mix", "rows", "masks", "rope", "dt_in")]
    s_dt_w = sem("s_dt_w")
    dt_split, dt_prod = sem("dt_split"), sem("dt_prod")
    s_x = [sem(f"s_x{c}") for c in range(4)]
    s_g_last, s_store = sem("s_g_last"), sem("s_store")
    landed = [sem(f"landed{i}") for i in range(RING)]
    hi_made = sem("hi_made")
    lo_made = sem("lo_made")
    used = sem("used")
    taken = [sem("taken0"), sem("taken1")]
    rows_t = sem("rows_t")
    set_up = sem("set_up")
    set_cv = sem("set_cv")
    expo = sem("expo")
    ts_t, ts_hi, ts_lo = sem("ts_t"), sem("ts_hi"), sem("ts_lo")
    sq_x, var_x, rstd_x = sem("sq_x"), sem("var_x"), sem("rstd_x")
    dt_v, dt_e, dt_mm, dt_dec = sem("dt_v"), sem("dt_e"), sem("dt_mm"), sem("dt_dec")
    conv_t, cv_made, conv_v, th_made = sem("conv_t"), sem("cv_made"), sem("conv_v"), sem("th_made")
    back_t, tm_made, score_mm, scan_v = sem("back_t"), sem("tm_made"), sem("score_mm"), sem("scan_v")
    mv_made, t2_made, seg_mm, ex_made = sem("mv_made"), sem("t2_made"), sem("seg_mm"), sem("ex_made")
    mw_made, mw_steps, dt_t, masks_made = sem("mw_made"), sem("mw_steps"), sem("dt_t"), sem("masks_made")
    st_mm, st_made, y_mm, off_mm = sem("st_mm"), sem("st_made"), sem("y_mm"), sem("off_mm")
    z_v, z_sq, z_root = sem("z_v"), sem("z_sq"), sem("z_root")
    r_sq, r_v, r_root, r_t, r_made = sem("r_sq"), sem("r_v"), sem("r_root"), sem("r_t"), sem("r_made")
    vg_made, at_sc, at_max, at_exp = sem("vg_made"), sem("at_sc"), sem("at_max"), sem("at_exp")
    at_v, at_t, at_pt, at_pv = sem("at_v"), sem("at_t"), sem("at_pt"), sem("at_pv")
    at_hi, at_lo, at_pt_lo, r_lo, r_cross = [
        sem(n) for n in ("at_hi", "at_lo", "at_pt_lo", "r_lo", "r_cross")]
    merge_v, hid_sq, fin_v, fin_a = sem("merge_v"), sem("hid_sq"), sem("fin_v"), sem("fin_a")

    CONV_V = 4 * TAPS + 1
    SCAN_V = 9
    Z_V = 7
    ROPE_V = 7
    AT_V = 3
    DT_A = 22

    def product(par, tb):
        return G[:, 2 * par + tb, :]

    def x_bank(j, c, part=slice(0, T)):
        bank = (S[:, 0:2, :], G[:, 2:4, :], S[:, 2:4, :])[j % 3]
        return bank[:, c // 2, c % 2 * T + part.start:c % 2 * T + part.stop]

    u_dt = tmp_a[:, :, :].rearrange("p b n -> p (b n)")[:, 0:6 * TB * DTW].rearrange(
        "p (m n) -> p m n", m=6)
    dt_rows = u_dt[0:DTW, 3:5, :].rearrange("p a b -> p (a b)")

    def done(r, par):
        return piece_number(r, par, PIECES)

    block = keep.enter_context(nc.Block())

    @block.sync
    def _(sp):
        w_in_k = w_in.rearrange("a (k p) n -> (a p) k n", p=P)
        mats = {"ssm_up": w_ssm_up, "attn_up": w_attn_up, "out": w_out, "mlp_in": w_mlp_in,
                "mlp_out": w_mlp_out}
        mats = {n: w.rearrange("a (k p) n -> (a p) k n", p=P) for n, w in mats.items()}
        cols = {"z": COL_Z, "k": COL_K, "v": COL_V, "q": COL_Q, "ga": COL_GA, "gb": COL_GB}

        x_k = x.rearrange("a (b p) n -> (a p) b n", p=P)
        for c in range(4):
            sp.dma_start(x_sb[:, :, c * N:(c + 1) * N], x_k[:, :, c * N:(c + 1) * N]).then_inc(s_x[c], 16)

        def parameters():
            for n, g in ((1, g_mlp), (2, ssm_norm_g)):
                sp.dma_start(param_rows[n * KT:(n + 1) * KT, 0, :],
                             g.rearrange("a (k p) -> (a k) p", p=P)).then_inc(s_rows, 16)
            taps = conv_w.rearrange("a t (k p) -> (a t k) p", p=P)
            rows = 2 * KT
            sp.dma_start(param_rows[:, 1, :], taps[0:3 * rows, :]).then_inc(s_rows, 16)
            sp.dma_start(param_rows[0:2 * rows, 2, :], taps[3 * rows:5 * rows, :]).then_inc(s_rows, 16)
            sp.dma_start(param_rows[2 * rows:3 * rows, 2, :],
                         conv_b.rearrange("a (k p) -> (a k) p", p=P)).then_inc(s_rows, 16)
            for n, (b, a) in enumerate(((dt_bias_f, a_log_f), (dt_bias_b, a_log_b))):
                sp.dma_start(dt_bias[:, n, :], b.to_broadcast([P, HEADS])).then_inc(s_dt_in, 16)
                sp.dma_start(exp_a[:, n, :], a.to_broadcast([P, HEADS])).then_inc(s_dt_in, 16)
            sp.dma_start(dskip[:, :], d_skip.to_broadcast([P, HEADS])).then_inc(s_dt_in, 16)
            sp.dma_start(masks[:, :, :].rearrange("p m n -> p (m n)"), consts[:, P:5 * P]).then_inc(s_masks, 16)
            sp.dma_start(rope_raw[:, :, :, :].rearrange("p a b n -> p (a b n)"),
                         consts[:, 5 * P:9 * P]).then_inc(s_rope, 16)
            for n, g in enumerate((q_norm_g, k_norm_g)):
                sp.dma_start(qk_gain[:, n, :], g.to_broadcast([P, AD])).then_inc(s_rope, 16)

        def window(r, par, kind, idx, sides):
            for p in range(PIECES):
                if isinstance(r, int) and (r, par, p) == (0, 0, 2):
                    sp.dma_start(dt_raw[:, :, :], w_in_k[:, :, COL_DT:COL_DT + DTW]).then_inc(s_dt_w, 16)
                if isinstance(r, int) and (r, par, p) == (0, 0, RING):
                    parameters()
                if kind == "mlp_in" and first(idx[0]) and (idx[1], p) == (0, 0):
                    sp.wait_ge(used, done(16, 1))
                    sp.dma_start(g_last[:, :], g_final.rearrange("(a n) -> a n", a=1).to_broadcast([P, D])
                                 ).then_inc(s_g_last, 16)
                dst = raw[:, p % RING, :].rearrange("p (k n) -> p k n", k=2)
                if not (isinstance(r, int) and piece_number(r, par, p) < RING):
                    sp.wait_ge(lo_made, piece_number(r, par, p) - RING + 1)
                if kind == "xbc" or (kind == "z" and idx == 0):
                    if kind == "xbc":
                        at, pair, step = idx * (2 * P) + COL_XS, idx * P + COL_B, COL_C - COL_B
                    else:
                        at, pair, step = COL_Z, COL_Z + 2 * P, P
                    sp.dma_start(dst[:, :, 0:2 * P], w_in_k[:, 2 * p:2 * p + 2, ds(at, 2 * P)]
                                 ).then_inc(landed[p % RING], 16)
                    for t in range(2):
                        sp.dma_start(dst[:, :, (2 + t) * P:(3 + t) * P],
                                     w_in_k[:, 2 * p:2 * p + 2, ds(pair + t * step, P)]
                                     ).then_inc(landed[p % RING], 16)
                    continue
                if kind == "mlp_in":
                    src = mats[kind][:, 2 * p:2 * p + 2, ds((idx[0] * 4 + idx[1]) * N, N)]
                elif kind == "mlp_out":
                    src = mats[kind][:, ds(idx[0] * KT + 2 * p, 2), idx[1] * N:(idx[1] + 1) * N]
                elif kind in mats:
                    src = mats[kind][:, 2 * p:2 * p + 2, ds(idx * N, N)]
                else:
                    src = w_in_k[:, 2 * p:2 * p + 2, ds(idx * N + cols[kind], N)]
                sp.dma_start(dst, src).then_inc(landed[p % RING], 16)

        walk(sp, window)
        o_k = out.rearrange("a (b p) n -> (a p) b n", p=P)
        for half in range(2):
            for tb in (1, 0):
                cols = slice(half * D // 2, (half + 1) * D // 2)
                if tb == 0:
                    sp.wait_ge(fin_a, half + 1)
                else:
                    sp.wait_ge(fin_v, 5 * TB + half + 1)
                sp.dma_start(o_k[:, tb, cols], fin[:, tb, cols]).then_inc(s_store, 16)
        sp.wait_ge(s_store, 16 * 2 * TB)

    @block.scalar
    def _(act):
        act.dma_start(ident[:, :], consts[:, 0:P]).then_inc(s_ident, 16)
        act.dma_start(param_rows[0:KT, 0, :], g_mix.rearrange("a (k p) -> (a k) p", p=P)).then_inc(s_g_mix, 16)

        def split(n, slot, width, arrived):
            act.wait_ge(landed[slot], arrived)
            if not isinstance(n, int) or n >= RING:
                act.wait_ge(used, n - RING + 1)
            act.activation(whi[:, slot, 0:width], raw[:, slot, 0:width], ACT.Copy).then_inc(hi_made, 1)

        def split_high(rnd, dst, k0, gain=None, factor=1.0):
            act.wait_ge(ts_t, rnd + 1)
            if gain is None:
                for c in range(2):
                    last = act.activation(dst[:, ds(k0 + 2 * c, 2), :],
                                          S[:, c, :].rearrange("p (c t) -> p c t", c=2), ACT.Copy,
                                          scale=factor)
            else:
                for c in range(4):
                    last = act.activation(dst[:, k0 + c, :], S[:, c // 2, c % 2 * T:(c % 2 + 1) * T],
                                          ACT.Copy, scale=gains[:, gain * KT + k0 + c:gain * KT + k0 + c + 1])
            last.then_inc(ts_hi, 1)

        act.wait_ge(expo, 1)
        act.activation(z_rs[:, :], minus_half[:, 0:4], ACT.Exp)
        act.wait_ge(set_up, 1)
        for j in range(4):
            act.wait_ge(ts_t, TS_X + j + 1)
            for c in range(4):
                k = 4 * j + c
                last = act.activation(a_hi[:, k, :], x_bank(j, c), ACT.Copy, scale=gains[:, k:k + 1])
            last.then_inc(ts_hi, 1)
            if j < LEAD_HI:
                split(piece_number(0, 0, j), j, 2 * N, landed_count(0, 0, j, True))

        def rates(p, _, pr, pp):
            if p == 1:
                act.wait_ge(s_dt_w, 16)
                act.activation(dt_hi[:, :, :], dt_raw[:, :, :], ACT.Copy).then_inc(dt_split, 1)
            if p in (2, 3):
                act.activation(squares[:, p - 2, :], x_sb[:, p - 2, :], ACT.Square,
                               accum_out=x_ss[:, p - 2:p - 1]).then_inc(sq_x, 1)
            if p == 4:
                act.wait_ge(dt_prod, 1)
                act.activation(dt_rows, S[0:DTW, 2, 0:T], ACT.Copy).then_inc(dt_e, 1)
            if p == 4:
                act.wait_ge(s_dt_in, 16 * 5)
                act.activation(exp_a[:, :, :], exp_a[:, :, :], ACT.Exp).then_inc(dt_e, 1)
                act.wait_ge(s_masks, 16)
                act.activation(masks_r[:, :, :], masks[:, 0:2, :], ACT.Copy).then_inc(masks_made, 1)
            if p == 7:
                act.wait_ge(dt_v, 4)
                act.activation(u_dt[:, 2, :], u_dt[:, 1, :], ACT.Exp).then_inc(dt_e, 1)

        def decays(p, _, pr, pp):
            if p == 4:
                act.wait_ge(dt_mm, 1)
                act.activation(dec[:, :, :].rearrange("p a b -> p (a b)"), S[:, 3, 0:4 * HEADS], ACT.Exp
                               ).then_inc(dt_dec, 1)

        def conv(p, g, pr, pp):
            if p == 0:
                act.wait_ge(used, done(pr, pp))
                act.wait_ge(rstd_x, 1)
                if not first(g):
                    act.wait_ge(conv_v, g * CONV_V)
                for tb in range(TB):
                    last = act.activation(xt[:, tb * N:(tb + 1) * N], product(pp, tb), ACT.Copy,
                                          scale=rstd[:, tb:tb + 1])
                last.then_inc(taken[pp], 1)
            if p == 2:
                act.wait_ge(conv_t, g + 1)
                for c in range(2):
                    act.activation(cv[:, 2 * c:2 * c + 2, TAPS // 2:TAPS // 2 + T],
                                   S[:, c, :].rearrange("p (c t) -> p c t", c=2), ACT.Copy
                                   ).then_inc(cv_made, 1)
            if p == 6:
                act.wait_ge(conv_v, g * CONV_V + (CONV_V - 1))
                act.activation(xt[:, :], acc[:, :, :].rearrange("p c t -> p (c t)"), ACT.Tanh
                               ).then_inc(th_made, 1)

        def scan(p, g, pr, pp):
            if p == 0:
                act.wait_ge(back_t, g + 1)
                if not first(g):
                    act.wait_ge(scan_v, g * SCAN_V)
                    act.wait_ge(t2_made, 2 * g)
                    act.wait_ge(y_mm, 2 * g)
                for tb in range(TB):
                    act.activation(tm[:, tb, :], S[:, 1 + 2 * tb, 0:3 * P], ACT.Copy).then_inc(tm_made, 1)
            if p in (2, 3):
                c = p - 2
                act.wait_ge(seg_mm, 2 * g + (c + 1))
                if not first(g):
                    act.wait_ge(scan_v, g * SCAN_V)
                act.activation(ex[:, c, :, :].rearrange("p h l -> p (h l)"), S[:, 2 + c, :], ACT.Exp
                               ).then_inc(ex_made, 1)
            if p == 4:
                act.wait_ge(st_mm, g + 1)
                if not first(g):
                    act.wait_ge(off_mm, g)
                act.activation(st[:, :, :].rearrange("p a b -> p (a b)"), S[:, 3, :], ACT.Copy
                               ).then_inc(st_made, 1)

        def zgate(p, j, pr, pp):
            if p == 0:
                act.wait_ge(used, done(pr, pp))
                act.wait_ge(ts_t, TS_Z + j)
                if j == 0:
                    act.wait_ge(mw_made, TB * GROUPS)
                for tb in range(TB):
                    act.activation(tmp_a[:, tb, :], product(pp, tb), ACT.Copy, scale=rstd[:, tb:tb + 1])
                for tb in range(TB):
                    last = act.activation(tmp_b[:, tb, :], product(pp, tb), ACT.Tanh,
                                          scale=half_rstd[:, tb:tb + 1])
                last.then_inc(taken[pp], 1)
            if p == 2:
                act.wait_ge(z_v, j * Z_V + 2)
                for tb in range(TB):
                    for gg in range(2):
                        act.activation(tmp_b[:, tb, gg * T:(gg + 1) * T], tmp_a[:, tb, gg * T:(gg + 1) * T],
                                       ACT.Square, scale=0.5,
                                       accum_out=z_ss[:, 2 * tb + gg:2 * tb + gg + 1]).then_inc(z_sq, 1)
            if p == 7:
                split_high(TS_Z + j, b_hi, 4 * j, gain=2)

        def rope(p, n, pr, pp):
            if p == 0:
                act.wait_ge(used, done(pr, pp))
                if not first(n):
                    act.wait_ge(r_v, n * ROPE_V)
                for tb in range(TB):
                    act.activation(tmp_b[:, tb, :], product(pp, tb), ACT.Square, scale=rstd[:, tb:tb + 1]
                                   ).then_inc(r_sq, 1)
            if p == 7:
                act.wait_ge(r_t, n + 1)
                if n >= 2:
                    act.wait_ge(at_sc, 4 * (n - 1))
                dst = qT_hi if n else kT_hi
                for c in range(2):
                    act.activation(dst[:, 2 * c:2 * c + 2, :], S[:, c, :].rearrange("p (c t) -> p c t", c=2),
                                   ACT.Copy).then_inc(r_made, 1)

        def values(p, n, pr, pp):
            if p == 0:
                act.wait_ge(used, done(pr, pp))
                for tb in range(TB):
                    last = act.activation(v_sb[:, tb, :, :].rearrange("p h d -> p (h d)"), product(pp, tb),
                                          ACT.Copy, scale=rstd[:, tb:tb + 1])
                last.then_inc(taken[pp], 1)

        def attend(p, g, pr, pp):
            def exps(h):
                act.wait_ge(at_max, 8 * g + 2 * h + 2)
                if g:
                    act.wait_ge(at_t, 4 * (g - 1) + h + 1)
                for tb in range(TB):
                    act.activation(prob[:, h, tb, :], S[:, h % 2, tb * T:(tb + 1) * T], ACT.Exp,
                                   bias=nb[:, h, tb:tb + 1], scale=SCALE,
                                   accum_out=den[:, h, tb:tb + 1]).then_inc(at_exp, 1)

            def copy_pt(h):
                act.wait_ge(at_t, 4 * g + h + 1)
                if 4 * g + h:
                    act.wait_ge(at_pv, 4 * g + h)
                act.activation(pT_hi[:, :, :].rearrange("p s l -> p (s l)"), S[:, 2, :], ACT.Copy
                               ).then_inc(at_pt, 1)

            def high(pair):
                act.wait_ge(at_pv, 4 * g + 2 * pair + 2)
                act.activation(c_hi[:, 4 * g + 2 * pair:4 * g + 2 * pair + 2, :],
                               S[:, 3, :].rearrange("p (c t) -> p c t", c=2), ACT.Copy).then_inc(at_hi, 1)

            if 3 <= p < 7:
                copy_pt(p - 3)
            if p == 5:
                high(0)
            if p < 4:
                exps(p)
            if p == 7:
                high(1)

        def gate(dst, pr, pp):
            act.wait_ge(used, done(pr, pp))
            for tb in range(TB):
                last = act.activation(dst[:, tb, :], product(pp, tb), ACT.Tanh, scale=half_rstd[:, tb:tb + 1])
            last.then_inc(taken[pp], 1)

        def gate_a(p, j, pr, pp):
            if p == 0:
                if first(j):
                    act.wait_ge(r_t, 5)
                else:
                    act.wait_ge(merge_v, j)
                gate(tmp_a, pr, pp)

        def gate_b(p, j, pr, pp):
            if p == 0:
                act.wait_ge(ts_t, j + TS_MERGED)
                gate(tmp_b, pr, pp)

        def merged(p, j, pr, pp):
            if p == 2:
                split_high(j + TS_MERGED, m_hi, j * 4, factor=0.5)

        def residual(p, j, pr, pp):
            if p == 2:
                split_high(TS_X2 + j, b_hi, 4 * j, gain=1)
                for tb in range(TB):
                    act.activation(tmp_a[:, tb, :], x_sb[:, tb, j * N:(j + 1) * N], ACT.Square,
                                   accum_out=rows_ss[:, tb, j:j + 1]).then_inc(sq_x, 1)

        def hidden(p, idx, pr, pp):
            g, j = idx
            if p == 0:
                act.wait_ge(used, done(pr, pp))
                act.wait_ge(rstd_x, 2)
                for tb in range(TB):
                    last = act.activation(tmp_a[:, tb, :], product(pp, tb), ACT.Relu,
                                          scale=rstd_mlp[:, tb:tb + 1])
                last.then_inc(taken[pp], 1)
                act.wait_ge(ts_t, g * 4 + (TS_HID + j))
                act.wait_ge(taken[pp], pr + 1)
                act.activation(tmp_b[:, :, :], tmp_a[:, :, :], ACT.Square).then_inc(hid_sq, 1)
            if p == 2:
                split_high(g * 4 + (TS_HID + j), a_hi, 4 * j)

        def final_squares(j, tb):
            part = slice(j * N, (j + 1) * N)
            act.activation(y_sb[:, tb, part], x_sb[:, tb, part], ACT.Square,
                           accum_out=rows_ss[:, tb, j:j + 1]).then_inc(sq_x, 1)

        def finish(p, j, pr, pp):
            if p == 1:
                act.wait_ge(taken[pp], pr + 1)
                for tb in range(TB):
                    final_squares(j, tb)

        table = {f.__name__: f for f in (rates, decays, conv, scan, zgate, rope, values, attend, gate_a, gate_b,
                                         merged, residual, hidden, finish)}

        def window(r, par, kind, idx, sides):
            for p in range(PIECES):
                q = p + LEAD_HI
                if not (isinstance(r, int) and 2 * r + par == U_END - 1 and q >= PIECES):
                    threes = kind == "xbc" or (kind == "z" and idx == 0 and q < PIECES)
                    split(piece_number(r, par, q), q % RING, 2 * N, landed_count(r, par, q, threes))
                for name, at in sides:
                    if name in table:
                        table[name](p, at, *previous(r, par))

        walk(act, window)
        for tb in range(TB):
            act.wait_ge(fin_v, 3 * TB + tb + 1)
            final_squares(3, tb)
        act.wait_ge(rstd_x, 3)
        act.wait_ge(fin_v, 5 * TB)
        for half in range(2):
            part = fin[:, 0, half * D // 2:(half + 1) * D // 2]
            act.activation(part, part, ACT.Copy, scale=rstd_out[:, 0:1]).then_inc(fin_a, 1)

    @block.vector
    def _(dve):
        def split(n, slot, width):
            dve.wait_ge(hi_made, n + 1)
            dve.tensor_tensor(wlo[:, slot, 0:width], raw[:, slot, 0:width],
                              whi[:, slot, 0:width].bitcast(F32), ALU.subtract).then_inc(lo_made, 1)

        def split_low(rnd, hi, lo, k0, gain=None, factor=1.0):
            dve.wait_ge(ts_hi, rnd + 1)
            if gain is None:
                for c in range(2):
                    last = dve.scalar_tensor_tensor(
                        out=lo[:, ds(k0 + 2 * c, 2), :], in0=S[:, c, :].rearrange("p (c t) -> p c t", c=2),
                        scalar=factor, in1=hi[:, ds(k0 + 2 * c, 2), :].bitcast(F32),
                        op0=ALU.mult, op1=ALU.subtract)
            else:
                for c in range(4):
                    k = gain * KT + k0 + c
                    last = dve.scalar_tensor_tensor(
                        out=lo[:, k0 + c, :], in0=S[:, c // 2, c % 2 * T:(c % 2 + 1) * T],
                        scalar=gains[:, k:k + 1], in1=hi[:, k0 + c, :].bitcast(F32),
                        op0=ALU.mult, op1=ALU.subtract)
            last.then_inc(ts_lo, 1)

        half = TAPS // 2
        dve.memset(cv[:, :, 0:half], 0.0).then_inc(set_cv, 1)
        dve.memset(cv[:, :, half + T:2 * half + T], 0.0).then_inc(set_cv, 1)
        dve.wait_ge(rows_t, 1)
        dve.tensor_copy(gains[:, 0:KT], G[:, 0, 0:KT]).then_inc(set_up, 1)
        dve.wait_ge(set_up, 1)

        def split_x(j):
            dve.wait_ge(ts_hi, TS_X + j + 1)
            for c in range(4):
                k = 4 * j + c
                last = dve.scalar_tensor_tensor(
                    out=a_lo[:, k, :], in0=x_bank(j, c), scalar=gains[:, k:k + 1],
                    in1=a_hi[:, k, :].bitcast(F32), op0=ALU.mult, op1=ALU.subtract)
            last.then_inc(ts_lo, 1)

        for j in range(3):
            split_x(j)
            if j < LEAD_LO:
                split(piece_number(0, 0, j), j, 2 * N)

        def rates(p, _, pr, pp):
            if p == 0:
                split_x(3)
            if p == 1:
                dve.wait_ge(dt_split, 1)
                dve.tensor_tensor(dt_lo[:, :, :], dt_raw[:, :, :], dt_hi[:, :, :].bitcast(F32), ALU.subtract
                                  ).then_inc(dt_split, 1)
            if p == 5:
                dve.wait_ge(rows_t, 2)
                dve.tensor_copy(gains[:, KT:3 * KT], S[:, 3, KT:3 * KT]).then_inc(set_up, 1)
                weights = S[:, 3, 3 * KT:3 * KT + 6 * 2 * KT].rearrange("p (t k) -> p t k", t=TAPS + 1)
                for c in range(4):
                    tiles = weights[:, :, c:2 * GROUPS:2] if c < 2 else weights[:, :, c * GROUPS:(c + 1) * GROUPS]
                    dve.tensor_scalar(cw[:, :, c, :].rearrange("p g t -> p t g"), tiles, 0.5, None, ALU.mult
                                      ).then_inc(set_up, 1)
            if p == 3:
                dve.wait_ge(s_rope, 16 * 3)
                for n in range(2):
                    gain = qk_gain[:, n, :]
                    dve.tensor_tensor(rope_t[:, n, 0, :, :], rope_raw[:, 0, :, :],
                                      gain.unsqueeze(1).to_broadcast([P, TB, AD]), ALU.mult
                                      ).then_inc(set_up, 1)
                    for e in range(2):
                        dve.tensor_tensor(
                            rope_t[:, n, 1, :, e:AD:2], rope_raw[:, 1, :, e:AD:2],
                            gain[:, 1 - e:AD:2].unsqueeze(1).to_broadcast([P, TB, AD // 2]), ALU.mult
                        ).then_inc(set_up, 1)
                dve.wait_ge(sq_x, TB)
                dve.tensor_scalar(x_var[:, :], x_ss[:, :], 1.0 / D, EPS, ALU.mult, ALU.add).then_inc(var_x, 1)
            if p == 6:
                dve.wait_ge(rstd_x, 1)
                dve.tensor_scalar(half_rstd[:, :], rstd[:, :], 0.5, None, ALU.mult).then_inc(var_x, 1)
                dve.wait_ge(s_dt_in, 16 * 5)
                dve.wait_ge(dt_t, 1)
                u, m = u_dt[:, 0, :], u_dt[:, 1, :]
                for tb in range(TB):
                    dve.scalar_tensor_tensor(
                        out=u[:, tb * DTW:(tb + 1) * DTW], in0=S[:, 2, T + tb * DTW:T + (tb + 1) * DTW],
                        scalar=rstd[:, tb:tb + 1], in1=dt_bias[:, :, :].rearrange("p a b -> p (a b)"),
                        op0=ALU.mult, op1=ALU.add).then_inc(dt_v, 1)
                dve.wait_ge(dt_v, 2)
                dve.tensor_scalar(m, u, -1.0, None, ALU.mult).then_inc(dt_v, 1)
                dve.wait_ge(dt_v, 3)
                dve.tensor_tensor(m, u, m, ALU.min).then_inc(dt_v, 1)

        def decays(p, _, pr, pp):
            if p == 0:
                u, m, e, t, sq, poly = (u_dt[:, n, :] for n in range(6))
                dve.wait_ge(dt_e, 3)
                dve.tensor_scalar(t, e, 2.0, None, ALU.add).then_inc(dt_v, 1)
                dve.wait_ge(dt_v, 5)
                dve.reciprocal(t, t).then_inc(dt_v, 1)
                dve.wait_ge(dt_v, 6)
                dve.tensor_tensor(t, t, e, ALU.mult).then_inc(dt_v, 1)
                dve.wait_ge(dt_v, 7)
                dve.tensor_tensor(sq, t, t, ALU.mult).then_inc(dt_v, 1)
                dve.wait_ge(dt_v, 8)
                dve.tensor_scalar(poly, sq, 1.0 / 15, None, ALU.mult).then_inc(dt_v, 1)
                for n, k in enumerate((13, 11, 9, 7, 5, 3)):
                    dve.wait_ge(dt_v, 9 + n)
                    dve.scalar_tensor_tensor(out=poly, in0=poly, scalar=1.0 / k, in1=sq,
                                             op0=ALU.add, op1=ALU.mult).then_inc(dt_v, 1)
                dve.wait_ge(dt_v, 15)
                dve.scalar_tensor_tensor(out=poly, in0=poly, scalar=1.0, in1=t,
                                         op0=ALU.add, op1=ALU.mult).then_inc(dt_v, 1)
                dve.tensor_scalar(m, u, 0.0, None, ALU.max).then_inc(dt_v, 1)
                dve.wait_ge(dt_v, 17)
                dve.scalar_tensor_tensor(out=dtv[:, :, :, :].rearrange("p b d h -> p (b d h)"), in0=poly,
                                         scalar=2.0, in1=m, op0=ALU.mult, op1=ALU.add).then_inc(dt_v, 1)
                dve.wait_ge(dt_v, 18)
                for tb in range(TB):
                    dve.scalar_tensor_tensor(out=av[:, tb, :, :], in0=dtv[:, tb, :, :], scalar=-1.0,
                                             in1=exp_a[:, :, :], op0=ALU.mult, op1=ALU.mult).then_inc(dt_v, 1)
                dve.wait_ge(dt_v, 20)
                dve.tensor_copy(av_hi[:, :, :, :], av[:, :, :, :]).then_inc(dt_v, 1)
                dve.wait_ge(dt_v, 21)
                dve.tensor_tensor(av_lo[:, :, :, :], av[:, :, :, :], av_hi[:, :, :, :].bitcast(F32), ALU.subtract
                                  ).then_inc(dt_v, 1)
            if p == 5:
                dve.wait_ge(dt_dec, 1)
                for c in range(TB):
                    dve.tensor_tensor(wdt[:, c, :], dtv[:, c, c, :], dec[:, c, :], ALU.mult).then_inc(dt_v, 1)

        def taps(g, pair):
            base = 2 * TAPS * pair
            for t in range(TAPS):
                for cc in range(2):
                    c = 2 * pair + cc
                    w = cw[:, ds(g, 1), c, t:t + 1].rearrange("p a b -> p (a b)")
                    bias = cw[:, ds(g, 1), c, TAPS:TAPS + 1].rearrange("p a b -> p (a b)")
                    if t == 0:
                        dve.tensor_scalar(acc[:, c, :], cv[:, c, 0:T], w, bias, ALU.mult, ALU.add
                                          ).then_inc(conv_v, 1)
                    else:
                        dve.wait_ge(conv_v, g * CONV_V + (base + 2 * t + cc - 1))
                        dve.scalar_tensor_tensor(out=acc[:, c, :], in0=cv[:, c, t:t + T], scalar=w,
                                                 in1=acc[:, c, :], op0=ALU.mult, op1=ALU.add
                                                 ).then_inc(conv_v, 1)

        def conv(p, g, pr, pp):
            if p == 2:
                if first(g):
                    dve.wait_ge(set_cv, 2)
                    dve.wait_ge(set_up, 6)
                dve.wait_ge(cv_made, 2 * g + 1)
                taps(g, 0)
            if p == 4:
                dve.wait_ge(cv_made, 2 * g + 2)
                taps(g, 1)
            if p == 6:
                dve.wait_ge(th_made, g + 1)
                if not first(g):
                    dve.wait_ge(off_mm, g)
                dve.scalar_tensor_tensor(out=cs[:, :, :].rearrange("p c t -> p (c t)"), in0=xt[:, :],
                                         scalar=1.0, in1=acc[:, :, :].rearrange("p c t -> p (c t)"),
                                         op0=ALU.add, op1=ALU.mult).then_inc(conv_v, 1)

        def scan(p, g, pr, pp):
            def step(n):
                return g * SCAN_V + n

            def heads(t, n):
                return t.unsqueeze(2).to_broadcast([P, 4, n])

            w = mw[:, 1 - pp, :, :, :]
            if p == 0:
                dve.wait_ge(score_mm, g + 1)
                for c in range(TB):
                    dve.wait_ge(mw_made, 2 * g + (c + 1))
                    dve.tensor_tensor(w[:, c, :, :], w[:, c, :, :],
                                      S[:, 0, c * P:(c + 1) * P].unsqueeze(1).to_broadcast([P, 4, P]), ALU.mult
                                      ).then_inc(scan_v, 1)
            if p == 1:
                dve.wait_ge(tm_made, 2 * g + 2)
                dve.wait_ge(dt_v, DT_A + 2)
                if not first(g):
                    dve.wait_ge(st_mm, g)
                for c in range(TB):
                    xs = tm[:, c, 0:4 * HD].rearrange("p (h d) -> p h d", h=4)
                    dve.tensor_tensor(xd[:, c, :, :], xs, heads(wdt[:, c, ds(g * 4, 4)], HD), ALU.mult
                                      ).then_inc(scan_v, 1)
            if p == 3:
                dve.wait_ge(scan_v, step(2))
                for c in range(TB):
                    dve.wait_ge(ex_made, 2 * g + (c + 1))
                    dve.tensor_tensor(w[:, c, :, :], w[:, c, :, :], ex[:, c, :, :], ALU.mult
                                      ).then_inc(scan_v, 1)
            if p == 6:
                dve.wait_ge(off_mm, g + 1)
                for_state = dec[:, 2:4, ds(g * 4, 4)].unsqueeze(3).to_broadcast([P, TB, 4, HD])
                dve.tensor_tensor(t1[:, :, :, :], S[:, 0, :].rearrange("p (c h d) -> p c h d", c=TB, h=4),
                                  for_state, ALU.mult).then_inc(scan_v, 1)
                dve.wait_ge(scan_v, step(7))
                dve.wait_ge(t2_made, 2 * g + 2)
                dve.tensor_tensor(t1[:, :, :, :], t1[:, :, :, :], t2[:, :, :, :], ALU.add).then_inc(scan_v, 1)
                dve.wait_ge(scan_v, step(8))
                dve.tensor_tensor(y_sb[:, :, ds(g * (4 * HD), 4 * HD)],
                                  S[:, 2, :].rearrange("p (c n) -> p c n", c=TB),
                                  t1[:, :, :, :].rearrange("p c h d -> p c (h d)"), ALU.add
                                  ).then_inc(scan_v, 1)

        def zgate(p, j, pr, pp):
            def step(n):
                return j * Z_V + n

            if p == 1:
                dve.wait_ge(taken[pp], pr + 1)
                dve.scalar_tensor_tensor(out=tmp_b[:, :, :], in0=tmp_b[:, :, :], scalar=1.0,
                                         in1=tmp_a[:, :, :], op0=ALU.add, op1=ALU.mult).then_inc(z_v, 1)
                dve.wait_ge(z_v, step(1))
                dve.wait_ge(scan_v, SCAN_V * (2 * j + 2))
                dve.tensor_tensor(tmp_a[:, :, :], tmp_b[:, :, :], y_sb[:, :, j * N:(j + 1) * N], ALU.mult
                                  ).then_inc(z_v, 1)
            if p == 3:
                dve.wait_ge(z_sq, 4 * (j + 1))
                dve.tensor_scalar(z_rs[:, :], z_ss[:, :], 1.0 / (4 * HD), EPS, ALU.mult, ALU.add
                                  ).then_inc(z_v, 1)
            if p == 4:
                dve.wait_ge(z_root, j + 1)
                for tb in range(TB):
                    for gg in range(2):
                        part = tmp_a[:, tb, gg * T:(gg + 1) * T]
                        dve.tensor_scalar(part, part, z_rs[:, 2 * tb + gg:2 * tb + gg + 1], 0.5,
                                          ALU.mult, ALU.mult).then_inc(z_v, 1)
            if p == 7:
                split_low(TS_Z + j, b_hi, b_lo, 4 * j, gain=2)

        def rope(p, n, pr, pp):
            qk = 0 if n else 1

            def step(k):
                return n * ROPE_V + k

            if p == 1:
                for tb in range(TB):
                    dve.wait_ge(r_sq, 2 * n + tb + 1)
                    dve.tensor_reduce(q_ss[:, tb, :], tmp_b[:, tb, :].rearrange("p (h d) -> p h d", h=4),
                                      AX_X, ALU.add).then_inc(r_v, 1)
                dve.wait_ge(r_v, step(2))
                dve.tensor_scalar(q_rs[:, :, :], q_ss[:, :, :], 1.0 / AD, EPS, ALU.mult, ALU.add
                                  ).then_inc(r_v, 1)
            if p == 2:
                dve.wait_ge(r_root, 2 * (n + 1))
                if first(n):
                    dve.wait_ge(ts_t, TS_MERGED)
                else:
                    dve.wait_ge(r_t, n)
                for tb in range(TB):
                    last = dve.tensor_tensor(tmp_a[:, tb, :].rearrange("p (h d) -> p h d", h=4),
                                             product(pp, tb).rearrange("p (h d) -> p h d", h=4),
                                             q_rs[:, tb, :].unsqueeze(2).to_broadcast([P, 4, AD]), ALU.mult)
                last.then_inc(taken[pp], 1)
            if p in (4, 5):
                tb = p - 4
                dve.wait_ge(taken[pp], pr + 1)
                own = tmp_a[:, tb, :].rearrange("p (h d) -> p h d", h=4)
                cross = tmp_b[:, tb, :].rearrange("p (h d) -> p h d", h=4)
                dve.wait_ge(r_cross, 4 * n + (2 * tb + 2))
                dve.tensor_tensor(own, own, rope_t[:, qk, 0, tb, :].unsqueeze(1).to_broadcast([P, 4, AD]),
                                  ALU.mult).then_inc(r_v, 1)
                dve.wait_ge(r_v, step(3 + 2 * tb + 1))
                dve.tensor_tensor(own, own, cross, ALU.add).then_inc(r_v, 1)
            if p == 7:
                hi, lo = (qT_hi, qT_lo) if n else (kT_hi, kT_lo)
                for c in range(2):
                    dve.wait_ge(r_made, 2 * n + c + 1)
                    dve.tensor_tensor(lo[:, 2 * c:2 * c + 2, :], S[:, c, :].rearrange("p (c t) -> p c t", c=2),
                                      hi[:, 2 * c:2 * c + 2, :].bitcast(F32), ALU.subtract).then_inc(r_lo, 1)

        def attend(p, g, pr, pp):
            def biggest(h):
                dve.wait_ge(at_sc, 4 * g + h + 1)
                dve.tensor_reduce(mx[:, h, :], S[:, h % 2, :].rearrange("p (b s) -> p b s", b=TB),
                                  AX_X, ALU.max).then_inc(at_max, 1)
                dve.wait_ge(at_max, 8 * g + 2 * h + 1)
                dve.tensor_scalar(nb[:, h, :], mx[:, h, :], -SCALE, None, ALU.mult).then_inc(at_max, 1)

            def normalise(h):
                dve.wait_ge(at_exp, 8 * g + 2 * h + 2)
                dve.reciprocal(rden[:, h, :], den[:, h, :]).then_inc(at_v, 1)
                dve.wait_ge(at_v, (4 * g + h) * AT_V + 1)
                for tb in range(TB):
                    dve.tensor_scalar(prob[:, h, tb, :], prob[:, h, tb, :], rden[:, h, tb:tb + 1], None,
                                      ALU.mult).then_inc(at_v, 1)

            def low_pt(h):
                dve.wait_ge(at_pt, 4 * g + h + 1)
                dve.tensor_tensor(pT_lo[:, :, :].rearrange("p s l -> p (s l)"), S[:, 2, :],
                                  pT_hi[:, :, :].rearrange("p s l -> p (s l)").bitcast(F32), ALU.subtract
                                  ).then_inc(at_pt_lo, 1)

            def low(pair):
                dve.wait_ge(at_hi, 2 * g + pair + 1)
                k = 4 * g + 2 * pair
                dve.tensor_tensor(c_lo[:, k:k + 2, :], S[:, 3, :].rearrange("p (c t) -> p c t", c=2),
                                  c_hi[:, k:k + 2, :].bitcast(F32), ALU.subtract).then_inc(at_lo, 1)

            if p < 4:
                biggest(p)
            if 3 <= p < 7:
                low_pt(p - 3)
            if 1 <= p < 5:
                normalise(p - 1)
            if p == 5:
                low(0)
            if p == 7:
                low(1)

        def gated(dst, pr, pp):
            dve.wait_ge(used, done(pr, pp))
            dve.wait_ge(taken[pp], pr)
            for tb in range(TB):
                last = dve.scalar_tensor_tensor(out=dst[:, tb, :], in0=dst[:, tb, :], scalar=1.0,
                                                in1=product(pp, tb), op0=ALU.add, op1=ALU.mult)
            last.then_inc(taken[pp], 1)

        def gated_a(p, j, pr, pp):
            if p == 0:
                gated(tmp_a, pr, pp)

        def merged(p, j, pr, pp):
            if p == 0:
                gated(tmp_b, pr, pp)
                dve.wait_ge(taken[pp], pr + 1)
                dve.tensor_tensor(tmp_b[:, :, :], tmp_b[:, :, :], tmp_a[:, :, :], ALU.add).then_inc(merge_v, 1)
            if p == 2:
                split_low(j + TS_MERGED, m_hi, m_lo, j * 4, factor=0.5)

        def add_product(j, pr, pp):
            dve.wait_ge(used, done(pr, pp))
            for tb in range(TB):
                part = x_sb[:, tb, j * N:(j + 1) * N]
                last = dve.tensor_tensor(part, part, product(pp, tb), ALU.add)
            last.then_inc(taken[pp], 1)

        def residual(p, j, pr, pp):
            if p == 0:
                add_product(j, pr, pp)
            if p == 2:
                split_low(TS_X2 + j, b_hi, b_lo, 4 * j, gain=1)
            if p == 4 and j == 3:
                dve.wait_ge(sq_x, 5 * TB)
                dve.tensor_reduce(x_ss[:, :], rows_ss[:, :, :], AX_X, ALU.add).then_inc(var_x, 1)
                dve.wait_ge(var_x, 3)
                dve.tensor_scalar(x_var[:, :], x_ss[:, :], 1.0 / D, EPS, ALU.mult, ALU.add).then_inc(var_x, 1)

        def hidden(p, idx, pr, pp):
            g, j = idx
            if p == 2:
                split_low(g * 4 + (TS_HID + j), a_hi, a_lo, 4 * j)

        def add(p, j, pr, pp):
            if p == 0:
                add_product(j, pr, pp)

        def times_gain(j, tb):
            part = slice(j * N, (j + 1) * N)
            dve.tensor_tensor(fin[:, tb, part], x_sb[:, tb, part], g_last[:, part], ALU.mult).then_inc(fin_v, 1)

        def finish(p, j, pr, pp):
            add(p, j, pr, pp)
            if p == 2:
                dve.wait_ge(taken[pp], pr + 1)
                dve.wait_ge(s_g_last, 16)
                for tb in range(TB):
                    times_gain(j, tb)

        table = {f.__name__: f for f in (rates, decays, conv, scan, zgate, rope, attend, gated_a, merged, residual,
                                         hidden, add, finish)}

        def window(r, par, kind, idx, sides):
            for p in range(PIECES):
                q = p + LEAD_LO
                if not (isinstance(r, int) and 2 * r + par == U_END - 1 and q >= PIECES):
                    split(piece_number(r, par, q), q % RING, 2 * N)
                for name, at in sides:
                    if name in table:
                        table[name](p, at, *previous(r, par))

        walk(dve, window)
        dve.wait_ge(used, done(U_END // 2 - 1, 1))
        for tb in range(TB):
            part = x_sb[:, tb, 3 * N:4 * N]
            dve.tensor_tensor(part, part, product(1, tb), ALU.add).then_inc(fin_v, 1)
        for tb in range(TB):
            dve.wait_ge(fin_v, 3 * TB + tb + 1)
            times_gain(3, tb)
        dve.wait_ge(sq_x, 9 * TB)
        dve.tensor_reduce(x_ss[:, :], rows_ss[:, :, :], AX_X, ALU.add).then_inc(var_x, 1)
        dve.wait_ge(var_x, 5)
        dve.tensor_scalar(x_var[:, :], x_ss[:, :], 1.0 / D, EPS, ALU.mult, ALU.add).then_inc(var_x, 1)
        dve.wait_ge(rstd_x, 3)
        for half in range(2):
            part = fin[:, 1, half * D // 2:(half + 1) * D // 2]
            dve.tensor_scalar(part, part, rstd_out[:, 1:2], None, ALU.mult).then_inc(fin_v, 1)

    @block.gpsimd
    def _(pool):
        pool.memset(minus_half[:, :], -0.5).then_inc(expo, 1)
        pool.wait_ge(expo, 1)

        def inverse_root(dst, src, n):
            return pool.tensor_tensor(dst, src, minus_half[:, 0:n], ALU.pow)

        def rates(p, _, pr, pp):
            if p == 2:
                pool.wait_ge(var_x, 1)
                inverse_root(rstd[:, :], x_var[:, :], TB).then_inc(rstd_x, 1)

        def masked_rates(g, c):
            for d in range(2):
                for part, rate in ((mv_hi, av_hi), (mv_lo, av_lo)):
                    pool.tensor_tensor(
                        part[:, c, d, :, :], masks[:, 2 + d, :].unsqueeze(1).to_broadcast([P, 4, P]),
                        rate[:, c, d, ds(g * 4, 4)].bitcast(F32).unsqueeze(2).to_broadcast([P, 4, P]), ALU.mult
                    ).then_inc(mv_made, 1)

        def masked_dt(g, parity, c):
            for d, dst in enumerate((mw[:, parity, c, :, :], mw_b)):
                pool.tensor_tensor(dst, masks[:, 2 + d, :].unsqueeze(1).to_broadcast([P, 4, P]),
                                   dtv[:, c, d, ds(g * 4, 4)].unsqueeze(2).to_broadcast([P, 4, P]), ALU.mult
                                   ).then_inc(mw_steps, 1)
            pool.wait_ge(mw_steps, 4 * g + (2 * c + 2))
            pool.tensor_tensor(mw[:, parity, c, :, :], mw[:, parity, c, :, :], mw_b, ALU.add
                               ).then_inc(mw_made, 1)

        def decays(p, _, pr, pp):
            if p == 0:
                pool.wait_ge(s_masks, 16)
                pool.wait_ge(dt_v, DT_A)
                for c in range(TB):
                    masked_rates(0, c)
                masked_dt(0, 0, 0)
                pool.wait_ge(mw_made, 1)
                masked_dt(0, 0, 1)

        def scan(p, g, pr, pp):
            if p == 0:
                pool.wait_ge(tm_made, 2 * g + 2)
                if not first(g):
                    pool.wait_ge(scan_v, g * SCAN_V)
                for c in range(TB):
                    pool.tensor_tensor(t2[:, c, :, :], tm[:, c, 0:4 * HD].rearrange("p (h d) -> p h d", h=4),
                                       dskip[:, ds(g * 4, 4)].unsqueeze(2).to_broadcast([P, 4, HD]), ALU.mult
                                       ).then_inc(t2_made, 1)
                if not (isinstance(g, int) and g == GROUPS - 1):
                    for c in range(TB):
                        pool.wait_ge(seg_mm, 2 * g + (c + 1))
                        masked_rates(g + 1, c)
                    if not first(g):
                        pool.wait_ge(y_mm, 2 * g)
                    for c in range(TB):
                        pool.wait_ge(mw_made, 2 * g + (c + 2))
                        masked_dt(g + 1, pp, c)

        def zgate(p, j, pr, pp):
            if p == 3:
                pool.wait_ge(z_v, j * Z_V + 3)
                inverse_root(z_rs[:, :], z_rs[:, :], 4).then_inc(z_root, 1)

        def rope(p, n, pr, pp):
            if p == 1:
                flat = q_rs[:, :, :].rearrange("p b h -> p (b h)")
                pool.wait_ge(r_v, n * ROPE_V + 3)
                inverse_root(flat, flat, 2 * 4).then_inc(r_root, 1)
                pool.wait_ge(r_root, 2 * n + 1)
                pool.tensor_tensor(q_rs[:, :, :], q_rs[:, :, :],
                                   rstd[:, :].unsqueeze(2).to_broadcast([P, TB, 4]), ALU.mult
                                   ).then_inc(r_root, 1)

            if p == 3:
                pool.wait_ge(taken[pp], pr + 1)
                for tb in range(TB):
                    own = tmp_a[:, tb, :].rearrange("p (h d) -> p h d", h=4)
                    cross = tmp_b[:, tb, :].rearrange("p (h d) -> p h d", h=4)
                    for e in range(2):
                        pool.tensor_tensor(
                            cross[:, :, e:AD:2], own[:, :, 1 - e:AD:2],
                            rope_t[:, 0 if n else 1, 1, tb, e:AD:2].unsqueeze(1).to_broadcast([P, 4, AD // 2]),
                            ALU.mult).then_inc(r_cross, 1)

        def attend(p, g, pr, pp):
            if p == 0:
                pool.wait_ge(taken[1], U_V // 2 + 1)
                if g:
                    pool.wait_ge(at_pv, 4 * g)
                pool.tensor_copy(vg_hi[:, :, :], v_sb[:, :, g, :]).then_inc(vg_made, 1)
                pool.wait_ge(vg_made, 2 * g + 1)
                pool.tensor_tensor(vg_lo[:, :, :], v_sb[:, :, g, :], vg_hi[:, :, :].bitcast(F32), ALU.subtract
                                   ).then_inc(vg_made, 1)

        def residual(p, j, pr, pp):
            if p == 4 and j == 3:
                pool.wait_ge(var_x, 4)
                inverse_root(rstd_mlp[:, :], x_var[:, :], TB).then_inc(rstd_x, 1)

        table = {f.__name__: f for f in (rates, decays, scan, zgate, rope, attend, residual)}

        def window(r, par, kind, idx, sides):
            for p in range(PIECES):
                for name, at in sides:
                    if name in table:
                        table[name](p, at, *previous(r, par))

        walk(pool, window)
        pool.wait_ge(var_x, 6)
        inverse_root(rstd_out[:, :], x_var[:, :], TB).then_inc(rstd_x, 1)

    @block.tensor
    def _(pe):
        operand = {"ssm_up": (b_hi, b_lo), "attn_up": (c_hi, c_lo), "out": (m_hi, m_lo),
                   "mlp_in": (b_hi, b_lo), "mlp_out": (a_hi, a_lo)}

        def three_passes(out_ap, k, tb, hi, lo, w_hi, w_lo, start, stop):
            cols = slice(tb * P, (tb + 1) * P)
            pe.matmul(out_ap, hi[:, k, cols], w_hi, start=start, stop=False)
            pe.matmul(out_ap, hi[:, k, cols], w_lo, start=False, stop=False)
            return pe.matmul(out_ap, lo[:, k, cols], w_hi, start=False, stop=stop)

        def transpose_round(src):
            for c in range(4):
                for tb in range(TB):
                    last = pe.transpose(S[:, c // 2, c % 2 * T + tb * P:c % 2 * T + (tb + 1) * P],
                                        src(c, tb), ident[:, :])
            return last

        def split_round(rnd, src):
            pe.wait_ge(ts_lo, rnd)
            transpose_round(src).then_inc(ts_t, 1)

        pe.wait_ge(s_ident, 16)
        for j in range(4):
            if j == 1:
                pe.wait_ge(s_g_mix, 16)
                pe.transpose(G[:, 0, 0:KT], param_rows[0:KT, 0, :], ident[0:KT, 0:KT]).then_inc(rows_t, 1)
            pe.wait_ge(s_x[j], 16)
            if j == 3:
                pe.wait_ge(ts_lo, TS_X + 1)
            for c in range(4):
                for tb in range(TB):
                    last = pe.transpose(x_bank(j, c, slice(tb * P, (tb + 1) * P)),
                                        x_sb[:, tb, (4 * j + c) * P:(4 * j + c + 1) * P], ident[:, :])
            last.then_inc(ts_t, 1)
        pe.wait_ge(set_up, 1)

        def rates(p, _, pr, pp):
            if p == 3:
                pe.wait_ge(dt_split, 2)
                pe.wait_ge(ts_lo, TS_X + 4)
                for k in range(KT):
                    into = S[0:DTW, 2, 0:T]
                    pe.matmul(into, dt_hi[:, k, :], a_hi[:, k, :], start=(k == 0), stop=False)
                    pe.matmul(into, dt_hi[:, k, :], a_lo[:, k, :], start=False, stop=False)
                    last = pe.matmul(into, dt_lo[:, k, :], a_hi[:, k, :], start=False, stop=(k == KT - 1))
                last.then_inc(dt_prod, 1)
            if p == 4:
                pe.wait_ge(s_rows, 16 * 5)
                at = 0
                for n, rows in enumerate((3 * KT, 6 * KT, 6 * KT)):
                    last = pe.transpose(S[:, 3, at:at + rows], param_rows[0:rows, n, :], ident[0:rows, 0:rows])
                    at += rows
                last.then_inc(rows_t, 1)
            if p == 5:
                pe.wait_ge(dt_e, 1)
                for tb in range(TB):
                    last = pe.transpose(S[:, 2, T + tb * DTW:T + (tb + 1) * DTW],
                                        dt_rows[:, tb * P:(tb + 1) * P], ident[0:DTW, 0:DTW])
                last.then_inc(dt_t, 1)

        def decays(p, _, pr, pp):
            if p == 3:
                pe.wait_ge(dt_v, DT_A)
                pe.wait_ge(s_masks, 16)
                pe.wait_ge(set_up, 6)
                for n, (m, c, d) in enumerate(((0, 0, 0), (1, 1, 1), (3, 0, 1), (2, 1, 0))):
                    last = pe.matmul(S[:, 3, n * HEADS:(n + 1) * HEADS], masks[:, m, :], av[:, c, d, :],
                                     start=True, stop=True)
                last.then_inc(dt_mm, 1)

        def conv(p, g, pr, pp):
            if p == 1:
                pe.wait_ge(taken[pp], pr + 1)
                if not first(g):
                    pe.wait_ge(scan_v, g * SCAN_V - SCAN_V + 2)
                    pe.wait_ge(tm_made, 2 * g)
                transpose_round(lambda c, tb: xt[:, tb * N + c * P:tb * N + (c + 1) * P]).then_inc(conv_t, 1)
            if p == 7:
                pe.wait_ge(conv_v, g * CONV_V + CONV_V)
                if first(g):
                    pe.wait_ge(dt_dec, 1)
                else:
                    pe.wait_ge(st_made, g)
                for tb in range(TB):
                    for c in range(3):
                        last = pe.transpose(S[:, 1 + 2 * tb, c * P:(c + 1) * P],
                                            cs[:, c, tb * P:(tb + 1) * P], ident[:, :])
                last.then_inc(back_t, 1)

        def scan(p, g, pr, pp):
            if p == 0:
                if not first(g):
                    pe.wait_ge(scan_v, g * SCAN_V)
                for c in range(TB):
                    last = pe.matmul(S[:, 0, c * P:(c + 1) * P], cs[:, 2, c * P:(c + 1) * P],
                                     cs[:, 3, c * P:(c + 1) * P], start=True, stop=True)
                last.then_inc(score_mm, 1)
            if p in (1, 2):
                c = p - 1
                pe.wait_ge(mv_made, 8 * g + (4 * c + 4))
                if c == 1:
                    pe.wait_ge(tm_made, 2 * g + 2)
                else:
                    pe.wait_ge(dt_v, 2)
                if first(g):
                    pe.wait_ge(masks_made, 1)
                for n in range(4):
                    d, part = n // 2, (mv_hi, mv_lo)[n % 2]
                    last = pe.matmul(S[:, 2 + c, :], masks_r[:, d, :],
                                     part[:, c, d, :, :].rearrange("p h l -> p (h l)"),
                                     start=(n == 0), stop=(n == 3))
                last.then_inc(seg_mm, 1)
            if p == 3:
                pe.wait_ge(scan_v, g * SCAN_V + 4)
                pe.wait_ge(ex_made, 2 * g + 2)
                for c in range(TB):
                    last = pe.matmul(S[:, 3, c * 4 * HD:(c + 1) * 4 * HD], tm[:, c, 2 * P:3 * P],
                                     xd[:, c, :, :].rearrange("p h d -> p (h d)"), start=True, stop=True)
                last.then_inc(st_mm, 1)
            if p in (4, 5):
                c = p - 4
                pe.wait_ge(scan_v, g * SCAN_V + (4 + (c + 1)))
                for h in range(4):
                    last = pe.matmul(S[:, 2, (4 * c + h) * HD:(4 * c + h + 1) * HD],
                                     mw[:, 1 - pp, c, h, :], tm[:, c, h * HD:(h + 1) * HD],
                                     start=True, stop=True)
                last.then_inc(y_mm, 1)
            if p == 5:
                pe.wait_ge(st_made, g + 1)
                if not (isinstance(g, int) and g == GROUPS - 1):
                    pe.wait_ge(cv_made, 2 * g + 3)
                for c in range(TB):
                    last = pe.matmul(S[:, 0, c * 4 * HD:(c + 1) * 4 * HD], cs[:, 3, c * P:(c + 1) * P],
                                     st[:, 1 - c, :], start=True, stop=True)
                last.then_inc(off_mm, 1)

        def zgate(p, j, pr, pp):
            if p == 6:
                pe.wait_ge(z_v, (j + 1) * Z_V)
                if j == 0:
                    pe.wait_ge(scan_v, SCAN_V * GROUPS)
                split_round(TS_Z + j, lambda c, tb: tmp_a[:, tb, c * P:(c + 1) * P])

        def rope(p, n, pr, pp):
            if p == 6:
                pe.wait_ge(r_v, (n + 1) * ROPE_V)
                if n == 0:
                    pe.wait_ge(ts_lo, TS_MERGED)
                else:
                    pe.wait_ge(r_lo, 2 * n)
                if n >= 2:
                    pe.wait_ge(at_exp, 8 * (n - 1))
                transpose_round(lambda c, tb: tmp_a[:, tb, c * P:(c + 1) * P]).then_inc(r_t, 1)

        def attend(p, g, pr, pp):
            def scores(h):
                pe.wait_ge(r_lo, 2 * (g + 2))
                if h >= 2:
                    pe.wait_ge(at_exp, 8 * g + 2 * (h - 1))
                for tb in range(TB):
                    last = three_passes(S[:, h % 2, tb * T:(tb + 1) * T], h, tb, qT_hi, qT_lo,
                                        kT_hi[:, g, :], kT_lo[:, g, :], True, True)
                last.then_inc(at_sc, 1)

            def turn(h):
                pe.wait_ge(at_v, (4 * g + h + 1) * AT_V)
                if 4 * g + h:
                    pe.wait_ge(at_pt_lo, 4 * g + h)
                for sb in range(TB):
                    for tb in range(TB):
                        last = pe.transpose(S[:, 2, sb * T + tb * P:sb * T + (tb + 1) * P],
                                            prob[:, h, tb, sb * P:(sb + 1) * P], ident[:, :])
                last.then_inc(at_t, 1)

            def weigh(h):
                pe.wait_ge(at_pt_lo, 4 * g + h + 1)
                pe.wait_ge(vg_made, 2 * g + 2)
                if 2 * g + h // 2:
                    pe.wait_ge(at_lo, 2 * g + h // 2)
                for sb in range(TB):
                    last = three_passes(S[:, 3, h % 2 * T:(h % 2 + 1) * T], sb, 0, vg_hi, vg_lo,
                                        pT_hi[:, sb, :], pT_lo[:, sb, :], sb == 0, sb == TB - 1)
                last.then_inc(at_pv, 1)

            if 3 <= p < 7:
                turn(p - 3)
            if p < 4:
                scores(p)
            if 4 <= p < 8:
                weigh(p - 4)

        def merged(p, j, pr, pp):
            if p == 1:
                pe.wait_ge(merge_v, j + 1)
                pe.wait_ge(at_exp, 8 * KVH)
                split_round(j + TS_MERGED, lambda c, tb: tmp_b[:, tb, c * P:(c + 1) * P])

        def residual(p, j, pr, pp):
            if p == 1:
                pe.wait_ge(taken[pp], pr + 1)
                split_round(TS_X2 + j, lambda c, tb: x_sb[:, tb, (4 * j + c) * P:(4 * j + c + 1) * P])

        def hidden(p, idx, pr, pp):
            g, j = idx
            if p == 1:
                pe.wait_ge(hid_sq, g * 4 + (j + 1))
                split_round(g * 4 + (TS_HID + j), lambda c, tb: tmp_b[:, tb, c * P:(c + 1) * P])

        table = {f.__name__: f for f in (rates, decays, conv, scan, zgate, rope, attend, merged, residual, hidden)}

        def window(r, par, kind, idx, sides):
            hi, lo = operand.get(kind, (a_hi, a_lo))
            if not (isinstance(r, int) and r == 0):
                pe.wait_ge(taken[par], r)
            rounds = {"ssm_up": TS_MERGED, "out": TS_X2, "mlp_in": TS_HID}.get(kind)
            if kind == "mlp_out":
                rounds = idx[0] * 4 + (TS_HID + 4)
            late = (kind == "out" and idx == 0) or (kind == "mlp_in" and first(idx[0]) and idx[1] == 0) or (
                kind == "mlp_out" and idx[1] == 0)
            for p in range(PIECES):
                if isinstance(r, int) and (r, par) == (0, 0) and p % 2 == 0:
                    pe.wait_ge(ts_lo, TS_X + p // 2 + 1)
                if p == 0 and rounds is not None:
                    pe.wait_ge(ts_lo, rounds - 1 if late else rounds)
                if p == PIECES - 2 and late:
                    pe.wait_ge(ts_lo, rounds)
                if p == 0 and kind == "attn_up":
                    pe.wait_ge(at_lo, 2 * KVH)
                pe.wait_ge(lo_made, piece_number(r, par, p) + 1)
                for kk in range(2):
                    k = 2 * p + kk
                    cols = slice(kk * N, (kk + 1) * N)
                    for tb in range(TB):
                        last = three_passes(product(par, tb), k, tb, hi, lo, whi[:, p % RING, cols],
                                            wlo[:, p % RING, cols], k == 0, k == KT - 1)
                last.then_inc(used, 1)
                for name, at in sides:
                    if name in table:
                        table[name](p, at, *previous(r, par))

        walk(pe, window)

    keep.close()


def shape_constants():
    grid_w, theta, half = 64, 10000.0, AD // 2
    i = np.arange(P)
    t, s = i[:, None], i[None, :]
    parts = [t == s, t > s, t < s, t <= s, t >= s]
    inv = (1.0 / (theta ** (np.arange(0, half, 2, dtype=np.float32) / np.float32(half)))).astype(np.float32)
    tok = np.arange(T)
    row, col = (tok // grid_w).astype(np.float32), (tok % grid_w).astype(np.float32)
    ang = np.concatenate([row[:, None] * inv, col[:, None] * inv], axis=1)
    cos = np.repeat(np.cos(ang), 2, axis=1)
    sin = np.stack([-np.sin(ang), np.sin(ang)], axis=-1).reshape(T, AD)
    for table in (cos, sin):
        parts += [table[:P], table[P:]]
    return np.concatenate([np.asarray(a, np.float32) for a in parts], axis=1)


_INS = ["x", "g_mix", "w_in", "conv_w", "conv_b", "dt_bias_f", "dt_bias_b", "a_log_f", "a_log_b", "d_skip",
        "ssm_norm_g", "q_norm_g", "k_norm_g", "w_ssm_up", "w_attn_up", "w_out", "g_mlp", "w_mlp_in",
        "w_mlp_out", "g_final"]


def kernel(**inputs):
    import concourse.bacc as bacc
    from concourse.bass_utils import run_bass_kernel_spmd

    nc = bacc.Bacc("TRN2", target_bir_lowering=False, num_devices=1)
    arrays, args = {}, []
    for name in _INS + ["consts"]:
        a = np.ascontiguousarray(shape_constants() if name == "consts" else inputs[name])
        arrays[f"in_{name}"] = a
        args.append(nc.dram_tensor(f"in_{name}", a.shape, mybir.dt.from_np(a.dtype), kind="ExternalInput").ap())
    out = nc.dram_tensor("out_0", (1, T, D), F32, kind="ExternalOutput").ap()
    build(nc, *args, out)
    r = run_bass_kernel_spmd(nc, [arrays], core_ids=[0])
    return r.results[0]["out_0"]
```
